# Optimizing a Trainium2 kernel written in Bass

```python
import math
import jax, jax.numpy as jnp
from jax import lax
import numpy as np

D_MODEL = 1024
BATCH = 1
SEQ = 128
DEPTH = 2
DEC_BATCH = 1
DEC_SEQ = 256
PAST_LEN = 128

GRID_W = 64
MOD_CHUNKS = 6
EPS = 1e-6
POOL_WIDTH = D_MODEL // 2
POOL_GROUPS = 4
POOL_GROUP_W = POOL_WIDTH // POOL_GROUPS
POOL_WINDOWS = (2, 4, 8, 16)
N_Q_HEADS = 8
N_KV_HEADS = 2
GQA_GROUP = N_Q_HEADS // N_KV_HEADS
HEAD_DIM = 64
ATTN_WIDTH = N_Q_HEADS * HEAD_DIM
KV_WIDTH = N_KV_HEADS * HEAD_DIM
WINDOW = 128
BLOCK = 128
ROPE_BASE = 10000.0
ATTN_SCALE = HEAD_DIM ** -0.5
SSD_HEADS = 16
SSD_HEADDIM = 64
SSD_INNER = SSD_HEADS * SSD_HEADDIM
SSD_GROUPS = 2
HEADS_PER_GROUP = SSD_HEADS // SSD_GROUPS
D_STATE = 128
CONV_W = 5
CHUNK = 128
CONV_CH = SSD_INNER + 2 * SSD_GROUPS * D_STATE
N_BRANCH = 3
D_FF = 4 * D_MODEL
IN_SIZES = (POOL_WIDTH, ATTN_WIDTH, KV_WIDTH, KV_WIDTH, SSD_INNER, CONV_CH, 2 * SSD_HEADS, N_BRANCH * D_MODEL)
IN_COLS = sum(IN_SIZES)

kernel_name = "hybrid_pool_swa_ssd_prefix_dit_step"

def rmsnorm(x, g):
    xf = x.astype(jnp.float32)
    y = xf * lax.rsqrt(jnp.mean(xf * xf, axis=-1, keepdims=True) + EPS)
    return (y * g.astype(jnp.float32)).astype(x.dtype)

def modulation(cvec, w_mod, b_mod):
    m = (jax.nn.silu(cvec) @ w_mod + b_mod)[..., None, :]
    return jnp.split(m, MOD_CHUNKS, axis=-1)

def in_projection(h, w_in):
    proj = h @ w_in
    offsets = []
    acc = 0
    for s in IN_SIZES[:-1]:
        acc += s
        offsets.append(acc)
    return jnp.split(proj, offsets, axis=-1)

def pool_mixer(u, pool_w, pool_scale):
    b, L, _ = u.shape
    cs = jnp.concatenate([jnp.zeros((b, 1, POOL_WIDTH), jnp.float32), jnp.cumsum(u.astype(jnp.float32), axis=1)], axis=1)
    t = jnp.arange(L)
    outs = []
    for gi, w in enumerate(POOL_WINDOWS):
        lo = jnp.clip(t - w // 2, 0, L)
        hi = jnp.clip(t + w // 2, 0, L)
        csg = cs[:, :, gi * POOL_GROUP_W:(gi + 1) * POOL_GROUP_W]
        cnt = (hi - lo).astype(jnp.float32)[None, :, None]
        outs.append((csg[:, hi] - csg[:, lo]) / cnt)
    pooled = jnp.concatenate(outs, axis=-1).astype(u.dtype) - u
    pooled = pooled.reshape(b, L, POOL_GROUPS, POOL_GROUP_W)
    mixed = jnp.einsum('blgc,gcd->blgd', pooled, pool_w).reshape(b, L, POOL_WIDTH)
    return mixed * pool_scale

def axial_rope(x):
    L = x.shape[1]
    rows = L // GRID_W
    row = jnp.repeat(jnp.arange(rows), GRID_W).astype(jnp.float32)
    col = jnp.tile(jnp.arange(GRID_W), rows).astype(jnp.float32)
    half = HEAD_DIM // 2
    nf = half // 2
    inv = ROPE_BASE ** (-jnp.arange(nf, dtype=jnp.float32) / nf)

    def rot(xa, pos):
        ang = pos[:, None] * inv[None, :]
        cos = jnp.cos(ang)[None, :, None, :]
        sin = jnp.sin(ang)[None, :, None, :]
        x1, x2 = xa[..., :nf], xa[..., nf:]
        return jnp.concatenate([x1 * cos - x2 * sin, x1 * sin + x2 * cos], axis=-1)

    xf = x.astype(jnp.float32)
    return jnp.concatenate([rot(xf[..., :half], row), rot(xf[..., half:], col)], axis=-1).astype(x.dtype)

def context_attention(q, k, v, sink):
    b, L = q.shape[:2]
    nb = L // BLOCK
    qb = q.reshape(b, nb, BLOCK, N_KV_HEADS, GQA_GROUP, HEAD_DIM).transpose(1, 0, 2, 3, 4, 5)
    sink_b = sink.astype(jnp.float32).reshape(1, N_KV_HEADS, GQA_GROUP, 1, 1)

    def one_block(qblk):
        s = jnp.einsum('bqkgd,bskd->bkgqs', qblk, k).astype(jnp.float32) * ATTN_SCALE
        m = jnp.maximum(jnp.max(s, axis=-1, keepdims=True), sink_b)
        p = jnp.exp(s - m)
        denom = jnp.sum(p, axis=-1, keepdims=True) + jnp.exp(sink_b - m)
        o = jnp.einsum('bkgqs,bskd->bqkgd', (p / denom).astype(v.dtype), v)
        return o.reshape(b, BLOCK, ATTN_WIDTH)

    out = lax.map(one_block, qb)
    return out.transpose(1, 0, 2, 3).reshape(b, L, ATTN_WIDTH)

def latent_attention(q, k, v, k_ctx, v_ctx, sink):
    b, L = q.shape[:2]
    nb = L // BLOCK
    qb = q.reshape(b, nb, BLOCK, N_KV_HEADS, GQA_GROUP, HEAD_DIM)
    pad = ((0, 0), (BLOCK, BLOCK), (0, 0), (0, 0))
    kp = jnp.pad(k, pad).reshape(b, nb + 2, BLOCK, N_KV_HEADS, HEAD_DIM)
    vp = jnp.pad(v, pad).reshape(b, nb + 2, BLOCK, N_KV_HEADS, HEAD_DIM)
    kw = jnp.concatenate([kp[:, :-2], kp[:, 1:-1], kp[:, 2:]], axis=2)
    vw = jnp.concatenate([vp[:, :-2], vp[:, 1:-1], vp[:, 2:]], axis=2)
    qpos = jnp.arange(nb)[:, None] * BLOCK + jnp.arange(BLOCK)[None, :]
    kpos = (jnp.arange(nb)[:, None] - 1) * BLOCK + jnp.arange(3 * BLOCK)[None, :]
    valid = (jnp.abs(qpos[:, :, None] - kpos[:, None, :]) <= WINDOW) & ((kpos >= 0) & (kpos < L))[:, None, :]
    s_loc = jnp.einsum('bnqkgd,bnskd->bnkgqs', qb, kw).astype(jnp.float32) * ATTN_SCALE
    s_loc = jnp.where(valid[None, :, None, None], s_loc, -jnp.inf)
    s_ctx = jnp.einsum('bnqkgd,bskd->bnkgqs', qb, k_ctx).astype(jnp.float32) * ATTN_SCALE
    sink_b = sink.astype(jnp.float32).reshape(1, 1, N_KV_HEADS, GQA_GROUP, 1, 1)
    m = jnp.maximum(jnp.maximum(jnp.max(s_loc, axis=-1, keepdims=True), jnp.max(s_ctx, axis=-1, keepdims=True)), sink_b)
    p_loc = jnp.exp(s_loc - m)
    p_ctx = jnp.exp(s_ctx - m)
    denom = jnp.sum(p_loc, axis=-1, keepdims=True) + jnp.sum(p_ctx, axis=-1, keepdims=True) + jnp.exp(sink_b - m)
    o = (jnp.einsum('bnkgqs,bnskd->bnqkgd', (p_loc / denom).astype(v.dtype), vw)
         + jnp.einsum('bnkgqs,bskd->bnqkgd', (p_ctx / denom).astype(v.dtype), v_ctx))
    return o.reshape(b, L, ATTN_WIDTH)

def depthwise_conv(u, w, bias):
    pad = CONV_W // 2
    out = lax.conv_general_dilated(u, w[:, None, :], window_strides=(1,), padding=((pad, pad),),
                                   dimension_numbers=('NWC', 'WIO', 'NWC'), feature_group_count=u.shape[-1])
    return out + bias

def ssd_chunked(x, dt, A, B, C, init_state):
    b, L = x.shape[:2]
    nc = L // CHUNK
    G, HG, P, N = SSD_GROUPS, HEADS_PER_GROUP, SSD_HEADDIM, D_STATE
    xc = x.astype(jnp.float32).reshape(b, nc, CHUNK, G, HG, P)
    dtc = dt.reshape(b, nc, CHUNK, G, HG)
    Bc = B.astype(jnp.float32).reshape(b, nc, CHUNK, G, N)
    Cc = C.astype(jnp.float32).reshape(b, nc, CHUNK, G, N)
    acum = jnp.moveaxis(jnp.cumsum(dtc * A.reshape(G, HG), axis=2), 2, -1)
    causal = jnp.tril(jnp.ones((CHUNK, CHUNK), dtype=bool))
    seg = jnp.where(causal, acum[..., :, None] - acum[..., None, :], -jnp.inf)
    cb = jnp.einsum('bcign,bcjgn->bcgij', Cc, Bc)
    w_intra = cb[:, :, :, None] * jnp.exp(seg)
    dtx = xc * dtc[..., None]
    y_diag = jnp.einsum('bcghij,bcjghp->bcighp', w_intra, dtx)
    decay_to_end = jnp.exp(acum[..., -1:] - acum)
    chunk_states = jnp.einsum('bcghj,bcjgn,bcjghp->bcghpn', decay_to_end, Bc, dtx)
    chunk_decay = jnp.exp(acum[..., -1])

    def step(S, inp):
        st, dec = inp
        return S * dec[..., None, None] + st, S

    S0 = init_state.astype(jnp.float32).reshape(b, G, HG, P, N)
    S_final, S_in = lax.scan(step, S0, (jnp.moveaxis(chunk_states, 1, 0), jnp.moveaxis(chunk_decay, 1, 0)))
    S_in = jnp.moveaxis(S_in, 0, 1)
    y_off = jnp.einsum('bcign,bcghpn,bcghi->bcighp', Cc, S_in, jnp.exp(acum))
    y = (y_diag + y_off).reshape(b, L, SSD_HEADS, P)
    return y, S_final.reshape(b, SSD_HEADS, P, N)

def ssd_mixer(z, xbc, dt_raw, init_f, init_b, p):
    b, L, _ = xbc.shape
    xbc = jax.nn.silu(depthwise_conv(xbc, p['conv_w'], p['conv_b']))
    xs, Bs, Cs = jnp.split(xbc, [SSD_INNER, SSD_INNER + SSD_GROUPS * D_STATE], axis=-1)
    x = xs.reshape(b, L, SSD_HEADS, SSD_HEADDIM)
    B = Bs.reshape(b, L, SSD_GROUPS, D_STATE)
    C = Cs.reshape(b, L, SSD_GROUPS, D_STATE)
    dtb = p['dt_bias'].astype(jnp.float32)
    A = -jnp.exp(p['a_log'].astype(jnp.float32))
    dt_f_raw, dt_b_raw = jnp.split(dt_raw.astype(jnp.float32), 2, axis=-1)
    dt_f = jax.nn.softplus(dt_f_raw + dtb[0])
    dt_b = jax.nn.softplus(dt_b_raw + dtb[1])
    y_f, s_f = ssd_chunked(x, dt_f, A[0], B, C, init_f)
    y_b, s_b = ssd_chunked(x[:, ::-1], dt_b[:, ::-1], A[1], B[:, ::-1], C[:, ::-1], init_b)
    y = y_f + y_b[:, ::-1] + p['d_skip'].astype(jnp.float32)[:, None] * x.astype(jnp.float32)
    y = y.reshape(b, L, SSD_INNER) * jax.nn.silu(z.astype(jnp.float32))
    return rmsnorm(y, p['ssd_norm_g']).astype(z.dtype), s_f, s_b

def token_mixers(h, p, ctx):
    b, L, _ = h.shape
    pool_u, q, k, v, z, xbc, dt_raw, gate_logits = in_projection(h, p['w_in'])
    pool_out = pool_mixer(pool_u, p['pool_w'], p['pool_scale'])
    q = rmsnorm(q.reshape(b, L, N_Q_HEADS, HEAD_DIM), p['q_norm_g'])
    k = rmsnorm(k.reshape(b, L, N_KV_HEADS, HEAD_DIM), p['k_norm_g'])
    v = v.reshape(b, L, N_KV_HEADS, HEAD_DIM)
    if ctx is None:
        attn_out = context_attention(q, k, v, p['attn_sink'])
        init_f = jnp.zeros((b, SSD_HEADS, SSD_HEADDIM, D_STATE), jnp.float32)
        init_b = init_f
    else:
        k_ctx, v_ctx, s_ctx = ctx
        attn_out = latent_attention(axial_rope(q), axial_rope(k), v, k_ctx, v_ctx, p['attn_sink'])
        init_f, init_b = s_ctx[:, 0], s_ctx[:, 1]
    ssd_out, s_f, s_b = ssd_mixer(z, xbc, dt_raw, init_f, init_b, p)
    g_pool, g_attn, g_ssd = jnp.split(jax.nn.sigmoid(gate_logits), N_BRANCH, axis=-1)
    merged = (g_pool * (pool_out @ p['w_pool_o']) + g_attn * (attn_out @ p['w_attn_o'])
              + g_ssd * (ssd_out @ p['w_ssd_o']))
    out = merged @ p['w_out']
    if ctx is None:
        return out, (k, v, jnp.stack([s_f, s_b], axis=1).astype(h.dtype))
    return out, None

def layer(x, cvec, p, ctx):
    sh1, sc1, g1, sh2, sc2, g2 = modulation(cvec, p['w_mod'], p['b_mod'])
    h = rmsnorm(x, p['norm1_g']) * (1.0 + sc1) + sh1
    mix, ctx_tensors = token_mixers(h, p, ctx)
    x = x + g1 * mix
    h = rmsnorm(x, p['norm2_g']) * (1.0 + sc2) + sh2
    x = x + g2 * (jnp.square(jax.nn.relu(h @ p['w_mlp1'])) @ p['w_mlp2'])
    return x, ctx_tensors

def setup_inputs(seed: int = 0) -> dict:
    key = jax.random.key(seed)
    ks = jax.random.split(key, 40)

    def nrm(k, shape, scale):
        return jax.random.normal(k, shape, jnp.float32) * scale

    dt_init = jnp.exp(jax.random.uniform(ks[30], (DEPTH, 2, SSD_HEADS), jnp.float32, math.log(1e-3), math.log(1e-1)))
    return {
        'x_prompt': nrm(ks[0], (BATCH, SEQ, D_MODEL), 1.0),
        'x_sample': nrm(ks[1], (DEC_BATCH, DEC_SEQ, D_MODEL), 1.0),
        'cache_k': nrm(ks[2], (DEC_BATCH, DEPTH, PAST_LEN, N_KV_HEADS, HEAD_DIM), 1.0),
        'cache_v': nrm(ks[3], (DEC_BATCH, DEPTH, PAST_LEN, N_KV_HEADS, HEAD_DIM), 1.0),
        'state_ssd': nrm(ks[4], (DEC_BATCH, DEPTH, 2, SSD_HEADS, SSD_HEADDIM, D_STATE), 0.1),
        'c': nrm(ks[5], (DEC_BATCH, D_MODEL), 1.0),
        'c_ctx': nrm(ks[6], (D_MODEL,), 1.0),
        'w_mod': nrm(ks[7], (DEPTH, D_MODEL, MOD_CHUNKS * D_MODEL), 0.5 * D_MODEL ** -0.5),
        'b_mod': nrm(ks[8], (DEPTH, MOD_CHUNKS * D_MODEL), 0.02),
        'norm1_g': 1.0 + nrm(ks[9], (DEPTH, D_MODEL), 0.02),
        'norm2_g': 1.0 + nrm(ks[10], (DEPTH, D_MODEL), 0.02),
        'w_in': nrm(ks[11], (DEPTH, D_MODEL, IN_COLS), D_MODEL ** -0.5),
        'pool_w': nrm(ks[12], (DEPTH, POOL_GROUPS, POOL_GROUP_W, POOL_GROUP_W), POOL_GROUP_W ** -0.5),
        'pool_scale': 1.0 + nrm(ks[13], (DEPTH, POOL_WIDTH), 0.02),
        'w_pool_o': nrm(ks[14], (DEPTH, POOL_WIDTH, D_MODEL), POOL_WIDTH ** -0.5),
        'q_norm_g': 1.0 + nrm(ks[15], (DEPTH, HEAD_DIM), 0.02),
        'k_norm_g': 1.0 + nrm(ks[16], (DEPTH, HEAD_DIM), 0.02),
        'attn_sink': nrm(ks[17], (DEPTH, N_Q_HEADS), 1.0),
        'w_attn_o': nrm(ks[18], (DEPTH, ATTN_WIDTH, D_MODEL), ATTN_WIDTH ** -0.5),
        'conv_w': nrm(ks[19], (DEPTH, CONV_W, CONV_CH), CONV_W ** -0.5),
        'conv_b': nrm(ks[20], (DEPTH, CONV_CH), 0.02),
        'dt_bias': dt_init + jnp.log(-jnp.expm1(-dt_init)),
        'a_log': jnp.log(jax.random.uniform(ks[21], (DEPTH, 2, SSD_HEADS), jnp.float32, 1.0, 16.0)),
        'd_skip': 1.0 + nrm(ks[22], (DEPTH, SSD_HEADS), 0.1),
        'ssd_norm_g': 1.0 + nrm(ks[23], (DEPTH, SSD_INNER), 0.02),
        'w_ssd_o': nrm(ks[24], (DEPTH, SSD_INNER, D_MODEL), SSD_INNER ** -0.5),
        'w_out': nrm(ks[25], (DEPTH, D_MODEL, D_MODEL), D_MODEL ** -0.5),
        'w_mlp1': nrm(ks[26], (DEPTH, D_MODEL, D_FF), D_MODEL ** -0.5),
        'w_mlp2': nrm(ks[27], (DEPTH, D_FF, D_MODEL), D_FF ** -0.5),
    }

def reference(x_prompt, x_sample, cache_k, cache_v, state_ssd, c, c_ctx, w_mod, b_mod, norm1_g, norm2_g,
              w_in, pool_w, pool_scale, w_pool_o, q_norm_g, k_norm_g, attn_sink, w_attn_o, conv_w, conv_b,
              dt_bias, a_log, d_skip, ssd_norm_g, w_ssd_o, w_out, w_mlp1, w_mlp2):
    y_prompt = x_prompt
    y_sample = x_sample
    ks_out, vs_out, ss_out = [], [], []
    for l in range(DEPTH):
        p = {
            'w_mod': w_mod[l], 'b_mod': b_mod[l], 'norm1_g': norm1_g[l], 'norm2_g': norm2_g[l],
            'w_in': w_in[l], 'pool_w': pool_w[l], 'pool_scale': pool_scale[l], 'w_pool_o': w_pool_o[l],
            'q_norm_g': q_norm_g[l], 'k_norm_g': k_norm_g[l], 'attn_sink': attn_sink[l], 'w_attn_o': w_attn_o[l],
            'conv_w': conv_w[l], 'conv_b': conv_b[l], 'dt_bias': dt_bias[l], 'a_log': a_log[l],
            'd_skip': d_skip[l], 'ssd_norm_g': ssd_norm_g[l], 'w_ssd_o': w_ssd_o[l], 'w_out': w_out[l],
            'w_mlp1': w_mlp1[l], 'w_mlp2': w_mlp2[l],
        }
        y_prompt, (k_l, v_l, s_l) = layer(y_prompt, c_ctx, p, None)
        ks_out.append(k_l)
        vs_out.append(v_l)
        ss_out.append(s_l)
        y_sample, _ = layer(y_sample, c, p, (cache_k[:, l], cache_v[:, l], state_ssd[:, l]))
    new_cache_k = jnp.stack(ks_out, axis=1)
    new_cache_v = jnp.stack(vs_out, axis=1)
    new_state_ssd = jnp.stack(ss_out, axis=1)
    return (y_prompt, y_sample, new_cache_k, new_cache_v, new_state_ssd)


_drawn_inputs = setup_inputs


def setup_inputs(seed=0):
    import zlib

    import numpy as np

    out = dict(_drawn_inputs(seed))
    spreads = {}
    factors = {'cache_k': 5.075,
     'cache_v': 4.065,
     'norm2_g': 4.562,
     'pool_scale': 8.0,
     'q_norm_g': 8.0,
     'k_norm_g': 2.754,
     'attn_sink': 8.0,
     'd_skip': 6.755,
     'ssd_norm_g': 8.0}
    for name, (base, spread) in spreads.items():
        noise = np.random.default_rng([zlib.crc32(name.encode()), seed]).standard_normal(out[name].shape)
        drawn = base * np.exp(spread * noise) if base else spread * noise
        out[name] = __import__('jax').numpy.asarray(drawn.astype(out[name].dtype))
    for name, factor in factors.items():
        out[name] = (out[name] * factor).astype(out[name].dtype)
    return out
```

```python
from contextlib import ExitStack

import numpy as np

import concourse.bass as bass
from concourse import mybir

F32 = mybir.dt.float32
F32R = mybir.dt.float32r
ALU = mybir.AluOpType
ACT = mybir.ActivationFunctionType
AX_X = mybir.AxisListType.X

P = 128
D = 1024
KT = D // P
DEPTH = 2
CTX = 128
LAT = 256
T = CTX + LAT
TT = T // P
EPS = 1e-6
HD = 64
NQ, NKV = 8, 2
NQK = NQ + NKV
SCALE = HD ** -0.5
NEG = -1e30
GRID_W = 64
ROPE_BASE = 10000.0
SH = 16
HG = 8
INNER = 1024
DFF = 4096
C_POOL, C_Q, C_K, C_Z = 0, 512, 1024, 1280
C_XBC = C_Z + INNER
C_DT = C_XBC + 1536
C_GATE = C_DT + 2 * SH
KVD_COLS = 256 + 2 * SH
WINDOWS = (2, 4, 8, 16)
CONV_W = 5
CPW = 2 + CTX + 2 + LAT + 2
CVW = CTX + 2 + LAT
PPW = 8 + CTX + 8 + LAT + 8
SEG = ((0, CTX), (CTX, T))

STAGES = (("mod1", 16, 1), ("kvd", 4, 3), ("q", 4, 3), ("xbc", 12, 2), ("pool", 4, 2), ("mod2", 32, 1),
          ("gpa", 4, 2), ("poa", 2, 2), ("gpb", 4, 2), ("pob", 2, 2), ("gaa", 4, 2), ("aoa", 2, 2),
          ("gab", 4, 2), ("aob", 2, 2), ("gsa", 4, 2), ("gsb", 4, 2), ("z", 8, 3), ("so", 8, 2),
          ("wo", 8, 2), ("mlp", 64, 2))
UNIT0, STEP0, STEPS_OF = {}, {}, {}
_u = _s = 0
for _name, _n, _k in STAGES:
    UNIT0[_name], STEP0[_name], STEPS_OF[_name] = _u, _s, _k
    _u, _s = _u + _n, _s + _n * _k
UNITS, STEPS = _u, _s
Q_UNITS, Q_STEPS = 16, 32
RAW = 8
WS = 4
STEP_PRIME = 2 * RAW
BANK_USES = (40, 40, 39, 35)
BANK_USES_Q = 4
DVE_LINKS = 140
POOL_LINKS = 10
POOL_BANK = (1, 2, 3, 1)
HID_PRIME = 2

CONST = {}
_c = 0
for _name, _n in (("ident", P), ("upper", P), ("lower", P), ("ones", P), ("mask1", P), ("mask2", P),
                  ("rope", 2 * 2 * HD), ("edge", 4 * 16), ("comb", 16), ("eps", 1)):
    CONST[_name] = (_c, _c + _n)
    _c += _n
CONST_COLS = _c


def constants():
    out = np.zeros((P, CONST_COLS), np.float32)
    r = np.arange(P)

    def put(name, value):
        a, b = CONST[name]
        out[:value.shape[0], a:b] = value.reshape(value.shape[0], -1)

    put("ident", np.eye(P, dtype=np.float32))
    put("upper", (r[:, None] <= r[None, :]).astype(np.float32))
    put("lower", (r[:, None] >= r[None, :]).astype(np.float32))
    put("ones", np.ones((P, P), np.float32))
    put("mask1", np.where(r[None, :] <= r[:, None], 0.0, NEG).astype(np.float32))
    put("mask2", np.where(r[None, :] >= r[:, None], 0.0, NEG).astype(np.float32))
    nf = HD // 4
    inv = (np.float32(ROPE_BASE) ** (-np.arange(nf, dtype=np.float32) / np.float32(nf))).astype(np.float32)
    rope = np.zeros((P, 2, 2, HD), np.float32)
    for t in range(2):
        pos = t * P + r
        for half, at in enumerate((pos // GRID_W, pos % GRID_W)):
            ang = at.astype(np.float32)[:, None] * inv[None, :]
            c, s = np.cos(ang), np.sin(ang)
            rope[:, t, 0, half * 32:half * 32 + 32] = np.concatenate([c, c], 1)
            rope[:, t, 1, half * 32:half * 32 + 32] = np.concatenate([-s, s], 1)
    put("rope", rope)
    edge = np.zeros((P, 4, 2, 8), np.float32)
    for g, w in enumerate(WINDOWS):
        for i in range(8):
            edge[:, g, 0, i] = w / (min(i + w // 2, CTX) - max(i - w // 2, 0))
            at = CTX - 8 + i
            edge[:, g, 1, i] = w / (min(at + w // 2, CTX) - max(at - w // 2, 0))
    put("edge", edge)
    put("eps", np.full((P, 1), EPS, np.float32))
    put("comb", np.kron(np.eye(8), [[1, 0], [0, 1], [1, 0], [0, 1]]).astype(np.float32))
    return out


def backbone_step(nc, consts, x_prompt, x_sample, cache_k, cache_v, state_ssd, c, c_ctx, w_mod, b_mod, norm1_g,
                  norm2_g, w_in, pool_w, pool_scale, w_pool_o, q_norm_g, k_norm_g, attn_sink, w_attn_o, conv_w,
                  conv_b, dt_bias, a_log, d_skip, ssd_norm_g, w_ssd_o, w_out, w_mlp1, w_mlp2,
                  y_prompt, y_sample, new_k, new_v, new_state):
    def rows(w):
        return w.rearrange("l k n -> (l k) n")

    w_mod_r, w_in_r, w_po_r, w_ao_r = rows(w_mod), rows(w_in), rows(w_pool_o), rows(w_attn_o)
    w_so_r, w_out_r, w_m1_r, w_m2_r = rows(w_ssd_o), rows(w_out), rows(w_mlp1), rows(w_mlp2)
    b_mod_r = b_mod.rearrange("l (r p) -> (l r) p", p=P)
    norm1_r = norm1_g.rearrange("l (r p) -> (l r) p", p=P)
    norm2_r = norm2_g.rearrange("l (r p) -> (l r) p", p=P)
    ssdg_r = ssd_norm_g.rearrange("l (r p) -> (l r) p", p=P)
    pscale_r = pool_scale.rearrange("l (r p) -> (l r) p", p=P)
    convw_r = conv_w.rearrange("l w (r p) -> (l w r) p", p=P)
    convb_r = conv_b.rearrange("l (r p) -> (l r) p", p=P)
    pool_w_r = pool_w.rearrange("l g c d -> (l g c) d")
    cache_k_r = cache_k.rearrange("b l s h d -> (b l s) (h d)")
    cache_v_r = cache_v.rearrange("b l s h d -> (b l s) (h d)")
    new_k_r = new_k.rearrange("b l s h d -> (b l s) (h d)")
    new_v_r = new_v.rearrange("b l s h d -> (b l s) (h d)")
    state_r = state_ssd.rearrange("b l e h p n -> (b l e h p) n")
    new_state_r = new_state.rearrange("b l e h p n -> (b l e h p) n")
    dtb_r = dt_bias.rearrange("l e h -> l (e h)")
    alog_r = a_log.rearrange("l e h -> l (e h)")

    with ExitStack() as ctx:
        def sb(name, shape, dt=F32):
            return ctx.enter_context(nc.sbuf_tensor(name, shape, dt))

        def sb_two_types(name, name_r, shape):
            offset = (nc.sbuf_base + 31) // 32 * 32
            return sb(name, shape), nc.alloc_sbuf_tensor_at(name_r, shape, F32R, offset=offset)

        def sem(name):
            return ctx.enter_context(nc.semaphore(name))

        slots = [sb_two_types(f"raw{i}", f"wlo{i}", [P, 1024]) for i in range(RAW)]
        raw, wlo = [r[:] for r, _ in slots], [w[:] for _, w in slots]
        whi = sb("whi", [P, WS, 1024], F32R)
        xT = sb("xT", [P, KT, T])
        def rows_of(name):
            t = sb(name, [P, KT, T], F32R)
            return [t[:, k, :] for k in range(KT)]

        ahi, alo = rows_of("ahi"), rows_of("alo")
        bhi = rows_of("bhi")
        blo = [sb(f"blo{k}", [P, T], F32R)[:] for k in range(4)]
        gate2_blo = [sb_two_types(f"gate2_{k}", f"blo{k}", [P, T]) for k in range(4, 8)]
        gate2 = [g[:] for g, _ in gate2_blo]
        blo += [lo[:] for _, lo in gate2_blo]
        arena_g = sb("arena_g", [P, 4 * T + KT * T])
        arena_s = sb("arena_s", [P, 7680])
        xbuf = sb("xbuf", [P, TT, INNER])
        bc_cm = sb("bc_cm", [P, 4, CVW])
        b_tm = sb("b_tm", [P, TT, 2 * P])
        cbs = sb("cbs", [P, TT, P])
        cst = sb("cst", [P, CONST_COLS])
        tri_r = sb("tri_r", [P, 2, P], F32R)
        mask_r = sb("mask_r", [P, 3, P], F32R)
        tb = sb("tb", [P, 4, 392])
        rows_a = sb("rows_a", [100, P])
        rows_b = sb("rows_b", [48, P])
        pcol = sb("pcol", [P, 148])
        pw = sb("pw", [P, 4, P])
        bcast = sb("bcast", [P, 216])
        kvc = sb("kvc", [P, 2, P])
        modc = sb("modc", [P, 48, 2])
        coef = sb("coef", [P, 2, KT, 2])
        csil = sb("csil", [P, 2, KT])
        c4 = sb("c4", [P, KT * 60], F32R)
        dts = sb("dts", [P, 14, TT * 2 * SH])
        adt_hi = sb("adt_hi", [P, TT * 2 * SH], F32R)
        adt_lo = sb("adt_lo", [P, TT * 2 * SH], F32R)
        nadt_hi = sb("nadt_hi", [P, TT * 2 * SH], F32R)
        nadt_lo = sb("nadt_lo", [P, TT * 2 * SH], F32R)
        small = sb("small", [P, 112])
        bank = [ctx.enter_context(nc.psum_tensor(f"bank{i}", [P, 512], F32)) for i in range(4)]
        seg_ps = ctx.enter_context(nc.psum_tensor("seg_ps", [P, 2, 512], F32))
        y_ps = ctx.enter_context(nc.psum_tensor("y_ps", [P, 2, 512], F32))
        aux = y_ps[:, 1, :]
        ybank = y_ps[:, 0, :]

        def const(name):
            a, b = CONST[name]
            return cst[:, a:b]

        ident, upper, lower, ones = const("ident"), const("upper"), const("lower"), const("ones")
        rope = const("rope").rearrange("p (t s d) -> p t s d", t=2, s=2)
        edge = const("edge").rearrange("p (g e i) -> p g e i", g=4, e=2)
        comb, eps = const("comb"), const("eps")
        tri = (upper, lower)
        crow = arena_s[0:16, 0:P]
        modrow = arena_s[0:32, 4096 + 4 * PPW:4096 + 4 * PPW + 512]
        gate = [arena_g[:, k * T:(k + 1) * T] for k in range(4)]
        merged = arena_g[:, 4 * T:].rearrange("p (k t) -> p k t", k=KT)
        qkv = arena_g[:, 0:2304].rearrange("p (t n) -> p t n", t=TT)
        rtmp = arena_g[:, 2304:4224].rearrange("p (t n) -> p t n", t=TT)
        ew = arena_s[:, 0:2048].rearrange("p (b h i) -> p b h i", b=2, h=HG)
        dtx = arena_s[:, 2048:3072].rearrange("p (d n) -> p d n", d=2)
        dtxd = arena_s[:, 3072:4096].rearrange("p (d n) -> p d n", d=2)
        st = arena_s[:, 4096:6144].rearrange("p (d n) -> p d n", d=4)
        stage = arena_s[:, 6144:7680].rearrange("p (d n) -> p d n", d=3)
        qT = arena_s[:, 0:1536].rearrange("p (h t) -> p h t", h=4)
        kT = arena_s[:, 1536:2560].rearrange("p (h t) -> p h t", h=2)
        prob = arena_s[:, 2560:3328].rearrange("p (h t) -> p h t", h=2)
        kdup = arena_s[:, 2560:3584].rearrange("p (n c) -> p n c", n=4)
        probT = arena_s[:, 3328:4096].rearrange("p (h t) -> p h t", h=2)
        pu = arena_s[:, 4096:4096 + 4 * PPW].rearrange("p (g t) -> p g t", g=4)
        pwin = arena_s[:, 4096 + 4 * PPW:4096 + 6 * PPW].rearrange("p (g t) -> p g t", g=2)
        cpad = arena_s[:, 6544:6544 + 2 * CPW].rearrange("p (j t) -> p j t", j=2)
        mtmp = tb[:, 2, 0:T]
        ytmp = tb[:].rearrange("p a b -> p (a b)")[:, 0:512]
        convw = pcol[:, 0:60].rearrange("p (w j) -> p w j", w=CONV_W)
        convb, n1col, n2col = pcol[:, 60:72], pcol[:, 72:80], pcol[:, 80:88]
        pscol, ssdcol, bmcol = pcol[:, 88:92], pcol[:, 92:100], pcol[:, 100:148]
        qg, kg, sink = bcast[:, 0:64], bcast[:, 64:128], bcast[:, 128:136]
        dtb, alog, dskip = bcast[:, 136:168], bcast[:, 168:200], bcast[:, 200:216]
        (dtr, dtv, dta, dte, dtw, dtl, dtm, dtd, dtf, adt, acs, eac, etot, wdec) = [dts[:, i] for i in range(14)]
        nsink, nmax, nbias, sadd, sexp = (small[:, 0:8], small[:, 8:10], small[:, 10:12], small[:, 12:14],
                                          small[:, 14:16])
        den, rden, ysum, yrs = small[:, 16:18], small[:, 18:20], small[:, 20:23], small[:, 24:27]
        ssq = small[:, 32:62]
        rsq = small[:, 64:94]

        raw_loaded = [sem(f"raw_loaded{i}") for i in range(RAW)]
        hi_ready, lo_ready, gemm_step = sem("hi_ready"), sem("lo_ready"), sem("gemm_step")
        bank_free = [sem(f"bank_free{i}") for i in range(4)]
        const_loaded, x_loaded, param_loaded = sem("const_loaded"), sem("x_loaded"), sem("param_loaded")
        tri_ready, ctrans, csil_ready, chi_ready, c4_ready = (sem("tri_ready"), sem("ctrans"), sem("csil_ready"),
                                                              sem("chi_ready"), sem("c4_ready"))
        xtrans, pads_zeroed = sem("xtrans"), sem("pads_zeroed")
        ptrans, pcol_ready = sem("ptrans"), sem("pcol_ready")
        sq_ready, sq_used, stats_ready, rstd_ready = sem("sq_ready"), sem("sq_used"), sem("stats_ready"), sem("rstd_ready")
        modrow_ready, modcol_done, modc_ready = sem("modrow_ready"), sem("modcol_done"), sem("modc_ready")
        t_ready, h_hi, h_ready = sem("t_ready"), sem("h_hi"), sem("h_ready")
        x_wo, x_mlp = sem("x_wo"), sem("x_mlp")
        qkv_ready, qksq_ready, qkn_ready, qkrot_half, qkrot_ready = (sem("qkv_ready"), sem("qksq_ready"),
                                                         sem("qkn_ready"), sem("qkrot_half"), sem("qkrot_ready"))
        qkT_done, qkT_ready = sem("qkT_done"), sem("qkT_ready")
        scores_ready, nbias_ready, probs_exp, sexp_ready, probs_ready = (sem("scores_ready"), sem("nbias_ready"),
                                                            sem("probs_exp"), sem("sexp_ready"), sem("probs_ready"))
        sadd_ready = sem("sadd_ready")
        pT_done, pT_ready, pv_done, attn_hi, attn_ready = (sem("pT_done"), sem("pT_ready"), sem("pv_done"),
                                                           sem("attn_hi"), sem("attn_ready"))
        cpad_ready, conv_ready, silu_ready, xtm_done, xtm_ready = (sem("cpad_ready"), sem("conv_ready"),
                                                   sem("silu_ready"), sem("xtm_done"), sem("xtm_ready"))
        pu_ready, pooled_ready, pmix_done, pmix_hi, pmix_ready = (sem("pu_ready"), sem("pooled_ready"),
                                                   sem("pmix_done"), sem("pmix_hi"), sem("pmix_ready"))
        dt_step, dt_act, adt_ready, cum_done, acs_ready, rem_ready, decay_ready, wdec_ready = (
            sem("dt_step"), sem("dt_act"), sem("adt_ready"), sem("cum_done"), sem("acs_ready"), sem("rem_ready"),
            sem("decay_ready"), sem("wdec_ready"))
        aux_done, aux_free = sem("aux_done"), sem("aux_free")
        cbm_ready, dtxd_ready, dtx_ready, xd_ready = sem("cbm_ready"), sem("dtxd_ready"), sem("dtx_ready"), sem("xd_ready")
        st_ready, stT_ready = sem("st_ready"), sem("stT_ready")
        seg_done, exp_ready, w_ready, ydiag_done, y_free = (sem("seg_done"), sem("exp_ready"), sem("w_ready"),
                                                            sem("ydiag_done"), sem("y_free"))
        state_loaded, state_staged, state_out = sem("state_loaded"), sem("state_staged"), sem("state_out")
        zs_ready, yz_ready, ysq_ready, yn_ready, ytrans, ssd_hi, ssd_ready = (sem("zs_ready"), sem("yz_ready"),
                          sem("ysq_ready"), sem("yn_ready"), sem("ytrans"), sem("ssd_hi"), sem("ssd_ready"))
        gate_ready, gated_ready, merged_step, merged_full, m_hi, m_ready = (sem("gate_ready"), sem("gated_ready"),
                          sem("merged_step"), sem("merged_full"), sem("m_hi"), sem("m_ready"))
        relu_ready, hid_hi, hid_ready = sem("relu_ready"), sem("hid_hi"), sem("hid_ready")
        root_ready, qkss_ready, qkroot_ready, yroot_ready = (sem("root_ready"), sem("qkss_ready"), sem("qkroot_ready"),
                                                             sem("yroot_ready"))
        hid_sq, kdup_ready, pwin_ready = sem("hid_sq"), sem("kdup_ready"), sem("pwin_ready")
        kv_out, out_staged, out_stored, ytm_done = sem("kv_out"), sem("out_staged"), sem("out_stored"), sem("ytm_done")
        dve_link, pool_link, sp_awake = sem("dve_link"), sem("pool_link"), sem("sp_awake")
        block = ctx.enter_context(nc.Block())

        def step_end(name, i, m=None):
            k = STEPS_OF[name]
            return STEP_PRIME + STEP0[name] + i * k + (k if m is None else m + 1)

        def unit_end(u):
            if u < 0:
                return STEP_PRIME + 2 * (u + 1)
            for name, n, k in STAGES:
                if u < UNIT0[name] + n:
                    return step_end(name, u - UNIT0[name])

        def raw_count(u):
            return u // RAW + 1 + len([v for v in range(UNIT0["kvd"], UNIT0["q"]) if v <= u and v % RAW == u % RAW])

        RAW_LOADS = [raw_count(UNITS - RAW + i) for i in range(RAW)]

        def tm_cols(i):
            return slice(i * P, (i + 1) * P)

        CV = ((0, P), (CTX + 2, CTX + 2 + P), (CTX + 2 + P, CVW))

        @block.sync
        def _(sp):
            sp.dma_start(cst[:], consts).then_inc(const_loaded, 16)
            sp.dma_start(crow[0:8, :], c_ctx.rearrange("(r p) -> r p", p=P)).then_inc(const_loaded, 16)
            sp.dma_start(crow[8:16, :], c.rearrange("b (r p) -> (b r) p", p=P)).then_inc(const_loaded, 16)
            sp.dma_start(xbuf[:, 0, :], x_prompt.rearrange("b s d -> (b s) d")).then_inc(x_loaded, 16)
            sp.dma_start(xbuf[:, 1:3, :], x_sample.rearrange("b (t s) d -> s (b t) d", s=P)).then_inc(x_loaded, 16)
            with sp.Fori(0, DEPTH) as l:
                def unit(u, src, width, first):
                    nk = src.shape[0] // P
                    sp.wait_ge(gemm_step, l * STEPS + unit_end(u - RAW))
                    if first:
                        sp.sem_inc(sp_awake, 1)
                    sp.dma_start(raw[u % RAW].rearrange("p (k n) -> p k n", k=1024 // width)[:, 0:nk, 0:src.shape[1]],
                                 src.rearrange("(k p) n -> p k n", p=P)).then_inc(raw_loaded[u % RAW], 16)

                def wide(name, i, w, k0, c0, cols=512):
                    unit(UNIT0[name] + i, w[bass.ds(k0, 256), c0:c0 + cols], 512, i < 8)

                def tall(name, i, w, k0, c0):
                    unit(UNIT0[name] + i, w[bass.ds(k0, 512), c0:c0 + 256], 256, i < 2)

                sp.wait_ge(ssd_ready, l * KT + 1)
                for n, (dst, src) in enumerate((
                        (rows_a[0:60, :], convw_r[bass.ds(l * 60, 60), :]),
                        (rows_a[60:72, :], convb_r[bass.ds(l * 12, 12), :]),
                        (rows_a[72:80, :], norm1_r[bass.ds(l * 8, 8), :]),
                        (rows_a[80:88, :], norm2_r[bass.ds(l * 8, 8), :]),
                        (rows_a[88:92, :], pscale_r[bass.ds(l * 4, 4), :]),
                        (rows_a[92:100, :], ssdg_r[bass.ds(l * 8, 8), :]),
                        (rows_b[:], b_mod_r[bass.ds(l * 48, 48), :]),
                        (pw[:], pool_w_r[bass.ds(l * 512, 512), :].rearrange("(g p) d -> p g d", p=P)),
                        (kvc[:, 0, :], cache_k_r[bass.ds(l * P, P), :]),
                        (kvc[:, 1, :], cache_v_r[bass.ds(l * P, P), :]),
                        (qg, q_norm_g[bass.ds(l, 1), :].to_broadcast([P, 64])),
                        (kg, k_norm_g[bass.ds(l, 1), :].to_broadcast([P, 64])),
                        (sink, attn_sink[bass.ds(l, 1), :].to_broadcast([P, 8])),
                        (dtb, dtb_r[bass.ds(l, 1), :].to_broadcast([P, 32])),
                        (alog, alog_r[bass.ds(l, 1), :].to_broadcast([P, 32])),
                        (dskip, d_skip[bass.ds(l, 1), :].to_broadcast([P, 16])))):
                    sp.dma_start(dst, src).then_inc(param_loaded, 16)
                for n in range(4):
                    for kq in range(4):
                        wide("mod1", 4 * n + kq, w_mod_r, l * D + kq * 256, n * 512)
                for kq in range(4):
                    u = UNIT0["kvd"] + kq
                    sp.wait_ge(gemm_step, l * STEPS + unit_end(u - RAW))
                    dst = raw[u % RAW].rearrange("p (k n) -> p k n", k=2)
                    src = w_in_r[bass.ds(l * D + kq * 256, 256), :].rearrange("(k p) n -> p k n", p=P)
                    sp.dma_start(dst[:, :, 0:256], src[:, :, C_K:C_K + 256]).then_inc(raw_loaded[u % RAW], 16)
                    sp.dma_start(dst[:, :, 256:KVD_COLS], src[:, :, C_DT:C_DT + 32]).then_inc(raw_loaded[u % RAW], 16)
                for kq in range(4):
                    wide("q", kq, w_in_r, l * D + kq * 256, C_Q)
                for b in range(6):
                    for kh in range(2):
                        tall("xbc", 2 * b + kh, w_in_r, l * D + kh * 512, C_XBC + b * 256)
                for b in range(2):
                    for kh in range(2):
                        tall("pool", 2 * b + kh, w_in_r, l * D + kh * 512, C_POOL + b * 256)
                for n in range(8):
                    for kq in range(4):
                        wide("mod2", 4 * n + kq, w_mod_r, l * D + kq * 256, (4 + n) * 512)
                sp.wait_ge(qkn_ready, l + 1)
                sp.dma_start(new_k_r[bass.ds(l * P, P), :], qkv[:, 0, 512:640]).then_inc(kv_out, 16)
                sp.dma_start(new_v_r[bass.ds(l * P, P), :], qkv[:, 0, 640:768]).then_inc(kv_out, 16)

                def load_states(g):
                    for e in range(2):
                        sp.dma_start(stage[:, 1 + e, :].rearrange("p (k n) -> p k n", k=4),
                                     state_r[bass.ds((l * 2 + e) * 1024 + g * 512, 512), :]
                                     .rearrange("(k p) n -> p k n", p=P)).then_inc(state_loaded, 16)

                def store_states(g):
                    for e in range(2):
                        sp.wait_ge(state_staged, (l * 2 + g) * 2 + e + 1)
                        sp.dma_start(new_state_r[bass.ds((l * 2 + e) * 1024 + g * 512, 512), :]
                                     .rearrange("(k p) n -> p k n", p=P),
                                     stage[:, 1 + e, :].rearrange("p (k n) -> p k n", k=4)).then_inc(state_out, 16)

                for name, w, col in (("gpa", w_in_r, C_GATE), ("poa", w_po_r, 0), ("gpb", w_in_r, C_GATE + 512),
                                     ("pob", w_po_r, 512), ("gaa", w_in_r, C_GATE + 1024), ("aoa", w_ao_r, 0),
                                     ("gab", w_in_r, C_GATE + 1536), ("aob", w_ao_r, 512),
                                     ("gsa", w_in_r, C_GATE + 2048), ("gsb", w_in_r, C_GATE + 2560)):
                    for b in range(2):
                        if w is w_in_r:
                            for kh in range(2):
                                tall(name, 2 * b + kh, w, l * D + kh * 512, col + b * 256)
                        else:
                            tall(name, b, w, l * 512, col + b * 256)
                    if name == "gpa":
                        sp.wait_ge(pmix_done, l * 4 + 4)
                        load_states(0)
                    if name == "gaa":
                        store_states(0)
                        sp.wait_ge(state_out, (l * 2 + 1) * 32 + 1)
                        sp.sem_inc(sp_awake, 1)
                        load_states(1)
                for n in range(2):
                    for kq in range(4):
                        wide("z", 4 * n + kq, w_in_r, l * D + kq * 256, C_Z + n * 512)
                store_states(1)
                for name, w in (("so", w_so_r), ("wo", w_out_r)):
                    for b in range(4):
                        for kh in range(2):
                            tall(name, 2 * b + kh, w, l * D + kh * 512, b * 256)
                with sp.Fori(0, 4) as q:
                    for j in range(Q_UNITS):
                        b, kh = (j % 8) // 2, j % 2
                        sp.wait_ge(gemm_step, l * STEPS + unit_end(UNIT0["mlp"] + j - RAW) + q * Q_STEPS)
                        if j % 8 == 0:
                            sp.sem_inc(sp_awake, 1)
                        if j < 8:
                            src = w_m1_r[bass.ds(l * D + kh * 512, 512), bass.ds(q * 1024 + b * 256, 256)]
                        else:
                            src = w_m2_r[bass.ds(l * DFF + q * 1024 + kh * 512, 512), b * 256:b * 256 + 256]
                        sp.dma_start(raw[j % RAW].rearrange("p (k n) -> p k n", k=4),
                                     src.rearrange("(k p) n -> p k n", p=P)).then_inc(raw_loaded[j % RAW], 16)
                sp.wait_ge(state_out, (l * 2 + 2) * 32 + 1)
                sp.sem_inc(sp_awake, 1)
                sp.wait_ge(kv_out, (l + 1) * 32)
                sp.sem_inc(sp_awake, 1)
            sp.wait_ge(out_staged, KT)
            sp.dma_start(y_prompt.rearrange("b s d -> (b s) d"), xbuf[:, 0, :]).then_inc(out_stored, 16)
            sp.dma_start(y_sample.rearrange("b (t s) d -> s (b t) d", s=P), xbuf[:, 1:3, :]).then_inc(out_stored, 16)
            sp.wait_ge(out_stored, 32)

        @block.tensor
        def _(pe):
            pe.sem_inc(gemm_step, STEP_PRIME)
            pe.wait_ge(const_loaded, 48)
            nc.tensor.transpose(aux[:, 0:16], crow, ident[0:16, 0:16]).then_inc(ctrans, 1)
            pe.wait_ge(x_loaded, 32)
            for k in range(KT):
                if k >= 4:
                    pe.wait_ge(x_mlp, k - 3)
                for t in range(TT):
                    last = nc.tensor.transpose(bank[k % 4][:, tm_cols(t)], xbuf[:, t, tm_cols(k)], ident)
                last.then_inc(xtrans, 1)
            pe.wait_ge(x_mlp, KT)
            pe.wait_ge(csil_ready, 1)
            pe.wait_ge(c4_ready, 2)
            pe.wait_ge(tri_ready, 4)

            with pe.Fori(0, DEPTH) as l:
                uses = [0, 0, 0, 0]

                def claim(b, extra=None):
                    value = l * BANK_USES[b] + uses[b] + 1
                    pe.wait_ge(bank_free[b], value if extra is None else value + extra)
                    uses[b] += 1

                def arrived(name, i, q=None):
                    value = l * UNITS + UNIT0[name] + i + 1
                    pe.wait_ge(lo_ready, value if q is None else value + q * Q_UNITS)

                def split(u):
                    return (whi[:, u % WS, :], wlo[u % RAW])

                def gemm_cm(name, i, b, hi, lo, k0, first, last, q=None):
                    u = UNIT0[name] + i
                    arrived(name, i, q)
                    uh, ul = (w.rearrange("p (k n) -> p k n", k=4) for w in split(u))
                    for m in range(2):
                        dst = bank[2 * (b % 2) + m][:, 0:T]
                        if first:
                            claim(2 * (b % 2) + m, None if q is None else q * BANK_USES_Q)
                        for k in range(4):
                            nc.tensor.matmul(dst, uh[:, k, tm_cols(m)], hi[k0 + k], start=first and k == 0, stop=False)
                            nc.tensor.matmul(dst, uh[:, k, tm_cols(m)], lo[k0 + k], start=False, stop=False)
                            ins = nc.tensor.matmul(dst, ul[:, k, tm_cols(m)], hi[k0 + k], start=False, stop=last and k == 3)
                        ins.then_inc(gemm_step, 1)

                def gemm_tm(name, i, kq, cols):
                    arrived(name, i)
                    uh, ul = (w.rearrange("p (k n) -> p k n", k=2)[:, :, 0:cols] for w in split(UNIT0[name] + i))
                    for t in range(TT):
                        dst = bank[t][:, 0:cols]
                        if kq == 0:
                            claim(t)
                        for k in range(2):
                            a = 2 * kq + k
                            nc.tensor.matmul(dst, ahi[a][:, tm_cols(t)], uh[:, k, :], start=kq == 0 and k == 0, stop=False)
                            nc.tensor.matmul(dst, alo[a][:, tm_cols(t)], uh[:, k, :], start=False, stop=False)
                            ins = nc.tensor.matmul(dst, ahi[a][:, tm_cols(t)], ul[:, k, :], start=False, stop=kq == 3 and k == 1)
                        ins.then_inc(gemm_step, 1)

                def gemm_mod(name, i):
                    n, kq = i // 4, i % 4
                    last = i == (15 if name == "mod1" else 31)
                    arrived(name, i)
                    if i == 0:
                        claim(0)
                    uh, ul = (w.rearrange("p (k n) -> p k n", k=2) for w in split(UNIT0[name] + i))
                    for k in range(2):
                        a = 60 * (2 * kq + k) + 28 - 4 * n
                        nc.tensor.matmul(bank[0][0:32, :], c4[:, a:a + 32], uh[:, k, :], start=i == 0 and k == 0, stop=False)
                        ins = nc.tensor.matmul(bank[0][0:32, :], c4[:, a:a + 32], ul[:, k, :], start=False, stop=last and k == 1)
                    ins.then_inc(gemm_step, 1)

                def mod_columns(part):
                    n, at = ((4, 384), (8, 416))[part]
                    pe.wait_ge(modrow_ready, l * 2 + part + 1)
                    for j in range(4):
                        ins = nc.tensor.matmul(aux[:, at + 2 * n * j:at + 2 * n * (j + 1)], modrow[0:4 * n, tm_cols(j)],
                                               comb[0:4 * n, 0:2 * n], start=True, stop=True, skip_group_check=True)
                    ins.then_inc(modcol_done, 1)

                def stats(norm, k_range=range(KT)):
                    for k in k_range:
                        pe.wait_ge(sq_ready, (l * 2 + norm) * KT + k + 1)
                        nc.tensor.matmul(ybank[:, 0:T], ones, tb[:, k % 2, 0:T], start=k == 0, stop=k == KT - 1)\
                            .then_inc(sq_used, 1)

                pe.wait_ge(param_loaded, (l + 1) * 16 * 16)
                nc.tensor.transpose(aux[:, 0:100], rows_a[:], ident[0:100, 0:100])
                nc.tensor.transpose(aux[:, 100:148], rows_b[:], ident[0:48, 0:48]).then_inc(ptrans, 1)
                for i in range(4):
                    gemm_mod("mod1", i)
                for k in range(KT):
                    stats(0, (k,))
                    gemm_mod("mod1", 4 + k)
                for i in range(12, 16):
                    gemm_mod("mod1", i)
                mod_columns(0)
                for kq in range(4):
                    pe.wait_ge(h_ready, l * 2 * KT + 2 * kq + 2)
                    gemm_tm("kvd", kq, kq, KVD_COLS)
                for kq in range(4):
                    gemm_tm("q", kq, kq, 512)

                def x_transposes(j):
                    pe.wait_ge(silu_ready, l * 12 + j + 1)
                    if j >= 2:
                        pe.wait_ge(xtm_ready, l * 10 + j - 1)
                    src = tb[:, 2 + j % 2, 0:CVW] if j < 8 else bc_cm[:, j - 8, :]
                    for t, (a, b) in enumerate(CV):
                        ins = nc.tensor.transpose(seg_ps[:, j % 2, tm_cols(t)], src[:, a:b], ident)
                    ins.then_inc(xtm_done, 1)

                for b in range(6):
                    for kh in range(2):
                        gemm_cm("xbc", 2 * b + kh, b, ahi, alo, 4 * kh, kh == 0, kh == 1)
                    if b >= 1:
                        x_transposes(2 * b - 2)
                        x_transposes(2 * b - 1)

                for b in range(2):
                    for kh in range(2):
                        gemm_cm("pool", 2 * b + kh, b, ahi, alo, 4 * kh, kh == 0, kh == 1)
                for i in range(8):
                    gemm_mod("mod2", i)

                pe.wait_ge(qkrot_ready, l + 1)
                pe.wait_ge(xtm_ready, l * 10 + 10)
                for t in range(TT):
                    if t >= 1:
                        pe.wait_ge(qkT_ready, l * 5 + t)
                    for hp in range(4):
                        ins = nc.tensor.transpose(seg_ps[:, 0, tm_cols(hp)], qkv[:, t, tm_cols(hp)], ident)
                    ins.then_inc(qkT_done, 1)
                for kv in range(2):
                    pe.wait_ge(qkT_ready, l * 5 + 3 + kv)
                    pe.wait_ge(kdup_ready, l * 4 + 4)
                    for n in range(4):
                        ins = nc.tensor.transpose(seg_ps[:, 1, tm_cols(n)], kdup[:, n, tm_cols(kv)], ident)
                    ins.then_inc(qkT_done, 1)
                pe.wait_ge(qkT_ready, l * 5 + 5)

                pairs = [(t, hp) for t in range(TT) for hp in range(4)]

                def scores(i):
                    t, hp = pairs[i]
                    a, b = (384, 512) if t == 0 else (0, 384)
                    if i >= 1:
                        pe.wait_ge(probs_exp, l * 24 + 2 * i)
                    for h in range(2):
                        part = slice(64 * h, 64 * h + 64)
                        dst = seg_ps[:, h, 0:b - a]
                        ins = nc.tensor.matmul(dst, qT[part, hp, tm_cols(t)], kT[part, hp // 2, a:b], start=True, stop=t == 0)
                        if t:
                            at = P if t == 1 else 0
                            ins = nc.tensor.matmul(dst[:, at:at + P], ident, const("mask1" if t == 1 else "mask2"),
                                                   start=False, stop=True)
                    ins.then_inc(scores_ready, 1)

                def prob_transposes(i):
                    t, hp = pairs[i]
                    pe.wait_ge(probs_ready, l * 12 + i + 1)
                    if i >= 1:
                        pe.wait_ge(attn_ready, l * 12 + i)
                    for h in range(2):
                        for n in range(1 if t == 0 else 3):
                            ins = nc.tensor.transpose(y_ps[:, h, tm_cols(n)], prob[:, h, tm_cols(n)], ident)
                    ins.then_inc(pT_done, 1)

                def pv(i):
                    t, hp = pairs[i]
                    pe.wait_ge(pT_ready, l * 12 + i + 1)
                    vcol = slice(640 + 64 * (hp // 2), 704 + 64 * (hp // 2))
                    vals = [qkv[:, 0, vcol]] if t == 0 else [qkv[:, 1, vcol], qkv[:, 2, vcol],
                                                            kvc[:, 1, 64 * (hp // 2):64 * (hp // 2) + 64]]
                    for h in range(2):
                        for n, v in enumerate(vals):
                            ins = nc.tensor.matmul(ybank[64 * h:64 * h + 64, 384:512], v, probT[:, h, tm_cols(n)],
                                                   start=n == 0, stop=n == len(vals) - 1)
                    ins.then_inc(pv_done, 1)

                def pool_mix(g):
                    b = POOL_BANK[g]
                    pe.wait_ge(pooled_ready, l * 4 + g + 1)
                    claim(b)
                    nc.tensor.matmul(bank[b][:, 0:CTX], pw[:, g, :], pu[:, g, 8:8 + CTX], start=True, stop=True,
                                     skip_group_check=True)
                    nc.tensor.matmul(bank[b][:, CTX:T], pw[:, g, :], pu[:, g, 16 + CTX:16 + T], start=True,
                                     stop=True, skip_group_check=True).then_inc(pmix_done, 1)

                scores(0)
                for i in range(12):
                    for j in range(2):
                        gemm_mod("mod2", 8 + 2 * i + j)
                    prob_transposes(i)
                    if i < 11:
                        scores(i + 1)
                    pv(i)
                    if i >= 8:
                        pool_mix(i - 8)
                mod_columns(1)

                pe.wait_ge(modc_ready, l * 2 + 2)
                pe.wait_ge(adt_ready, l + 1)
                for t in range(TT):
                    for e in range(2):
                        at = t * 32 + e * 16
                        nc.tensor.matmul(aux[:, at:at + 16], tri[e], adt[:, at:at + 16], start=True, stop=True,
                                         skip_group_check=True)
                ins = nc.tensor.matmul(aux[:, 96:192], ones, adt, start=True, stop=True, skip_group_check=True)
                ins.then_inc(cum_done, 1)
                pe.wait_ge(decay_ready, l + 1)

                fillers = []
                for name, src_hi, src_lo, n_k in (("gpa", ahi, alo, 2), ("poa", bhi, blo, 1), ("gpb", ahi, alo, 2),
                                                  ("pob", bhi, blo, 1), ("gaa", ahi, alo, 2), ("aoa", bhi, blo, 1),
                                                  ("gab", ahi, alo, 2), ("aob", bhi, blo, 1), ("gsa", ahi, alo, 2),
                                                  ("gsb", ahi, alo, 2)):
                    for b in range(2):
                        for kh in range(n_k):
                            fillers.append((name, n_k * b + kh, b, src_hi, src_lo,
                                            4 * kh + (4 if name[0:2] == "ao" else 0), kh == 0, kh == n_k - 1))
                filled = [0]

                def fill(n=1):
                    for _ in range(n):
                        name, i, b, hi, lo, k0, first, last = fillers[filled[0]]
                        if name == "poa" and i == 0:
                            pe.wait_ge(pmix_ready, l * 4 + 4)
                        if name == "aoa" and i == 0:
                            pe.wait_ge(attn_ready, l * 12 + 12)
                        gemm_cm(name, i, b, hi, lo, k0, first, last)
                        filled[0] += 1

                def single(g, n):
                    if n or g:
                        pe.wait_ge(aux_free, (l * 2 + g) * 13 + n)

                def seg(g, i, t, e):
                    if i or g:
                        pe.wait_ge(exp_ready, (l * 2 + g) * 6 + i)
                    if i == 0 and g == 0:
                        pe.wait_ge(probs_exp, l * 24 + 24)
                    m = tri_r[:, e, :]
                    for half in range(2):
                        a = t * 32 + e * 16 + g * 8 + half * 4
                        dst = seg_ps[:, half, :].rearrange("p (h i) -> p h i", h=4)
                        nc.tensor.matmul(dst, mask_r[:, 0, :], mask_r[:, 2 - e, :].unsqueeze(1).to_broadcast([P, 4, P]),
                                         start=True, stop=False, skip_group_check=True)
                        for part in (nadt_hi, nadt_lo):
                            nc.tensor.matmul(dst, m, part[:, a:a + 4].unsqueeze(2).to_broadcast([P, 4, P]), start=False,
                                             stop=False, skip_group_check=True)
                        for h in range(4):
                            for n, part in enumerate((adt_hi, adt_lo)):
                                ins = nc.tensor.matmul(dst[:, h], part[:, a + h:a + h + 1].to_broadcast([P, P]), m,
                                                       start=False, stop=h == 3 and n == 1, skip_group_check=True)
                    ins.then_inc(seg_done, 1)

                def ydiag(g, t, e):
                    pe.wait_ge(w_ready, (l * 2 + g) * 6 + 2 * t + e + 1)
                    if e == 0:
                        pe.wait_ge(dtx_ready, (l * 2 + g) * 3 + t + 1)
                        if t or g:
                            pe.wait_ge(y_free, (l * 2 + g) * 3 + t)
                    for h in range(HG):
                        ins = nc.tensor.matmul(ybank[:, h * 64:h * 64 + 64], ew[:, e, h, :], dtx[:, e, h * 64:h * 64 + 64],
                                               start=h == 0 and e == 0, stop=h == 7 and e == 1, skip_group_check=True)
                    ins.then_inc(ydiag_done, 1)

                for g in range(2):
                    def state_sum(n, t):
                        single(g, n)
                        pe.wait_ge(dtxd_ready, (l * 2 + g) * 4 + {3: 1, 4: 2, 5: 3, 7: 4}[n])
                        nc.tensor.matmul(aux, b_tm[:, t, tm_cols(g)], dtxd[:, {3: 0, 4: 1, 5: 0, 7: 1}[n], :],
                                         start=True, stop=True).then_inc(aux_done, 1)

                    def transposes4(n, src):
                        single(g, n)
                        for j in range(4):
                            ins = nc.tensor.transpose(aux[:, tm_cols(j)], src[:, tm_cols(j)], ident)
                        ins.then_inc(aux_done, 1)

                    def yoff(n, t, e, s):
                        single(g, n)
                        a, b = CV[t]
                        nc.tensor.matmul(aux, bc_cm[:, 2 + g, a:b], st[:, s, :], start=True, stop=True).then_inc(aux_done, 1)

                    single(g, 0)
                    for t, (a, b) in enumerate(CV):
                        ins = nc.tensor.matmul(aux[:, tm_cols(t)], bc_cm[:, g, a:b], bc_cm[:, 2 + g, a:b], start=True, stop=True,
                                               skip_group_check=True)
                    ins.then_inc(aux_done, 1)
                    seg(g, 0, 0, 0)
                    fill()
                    pe.wait_ge(state_loaded, (l * 2 + g + 1) * 32)
                    transposes4(1, stage[:, 1])
                    seg(g, 1, 0, 1)
                    fill()
                    transposes4(2, stage[:, 2])
                    ydiag(g, 0, 0)
                    seg(g, 2, 1, 0)
                    fill()
                    ydiag(g, 0, 1)
                    state_sum(3, 2)
                    fill()
                    state_sum(4, 1)
                    seg(g, 3, 1, 1)
                    fill()
                    state_sum(5, 0)
                    ydiag(g, 1, 0)
                    fill(2)
                    pe.wait_ge(stT_ready, (l * 2 + g) * 2 + 1)
                    transposes4(6, stage[:, 0])
                    seg(g, 4, 2, 0)
                    fill()
                    ydiag(g, 1, 1)
                    state_sum(7, 0)
                    fill(2)
                    pe.wait_ge(stT_ready, (l * 2 + g) * 2 + 2)
                    transposes4(8, stage[:, 0])
                    seg(g, 5, 2, 1)
                    fill()
                    ydiag(g, 2, 0)
                    yoff(9, 1, 0, 0)
                    fill()
                    yoff(10, 1, 1, 3)
                    fill()
                    ydiag(g, 2, 1)
                    yoff(11, 2, 0, 2)
                    fill()
                    yoff(12, 2, 1, 1)
                    fill(2)

                for n in range(2):
                    for kq in range(4):
                        gemm_tm("z", 4 * n + kq, kq, 512)
                pe.wait_ge(yn_ready, l * TT + TT)
                pe.wait_ge(exp_ready, (l + 1) * 12)
                pe.wait_ge(aux_free, (l + 1) * 26)
                spare = (seg_ps[:, 0, :], seg_ps[:, 1, :], ybank, aux)
                for k in range(KT):
                    if k >= 4:
                        pe.wait_ge(ssd_ready, l * KT + 1 + k - 3)
                    for t in range(TT):
                        ins = nc.tensor.transpose(spare[k % 4][:, tm_cols(t)], xbuf[:, t, tm_cols(k)], ident)
                    ins.then_inc(ytrans, 1)
                for b in range(4):
                    for kh in range(2):
                        if b == 0:
                            pe.wait_ge(ssd_ready, l * KT + 1 + 4 * kh + 4)
                        gemm_cm("so", 2 * b + kh, b, ahi, alo, 4 * kh, kh == 0, kh == 1)
                for b in range(4):
                    for kh in range(2):
                        if b == 0:
                            pe.wait_ge(m_ready, l * KT + 4 * kh + 4)
                        gemm_cm("wo", 2 * b + kh, b, bhi, blo, 4 * kh, kh == 0, kh == 1)
                    if b >= 1:
                        stats(1, (2 * b - 2, 2 * b - 1))
                stats(1, (6, 7))
                base = list(uses)
                with pe.Fori(0, 4) as q:
                    uses[:] = base
                    for b in range(4):
                        for kh in range(2):
                            if b == 0:
                                pe.wait_ge(h_ready, l * 2 * KT + KT + 4 * kh + 4)
                            gemm_cm("mlp", 2 * b + kh, b, ahi, alo, 4 * kh, kh == 0, kh == 1, q)
                    for b in range(4):
                        for kh in range(2):
                            if b == 0:
                                pe.wait_ge(hid_ready, (l * 4 + q) * KT + HID_PRIME + 4 * kh + 4)
                            gemm_cm("mlp", 8 + 2 * b + kh, b, bhi, blo, 4 * kh, kh == 0, kh == 1, q)

            pe.wait_ge(x_mlp, (DEPTH * 4 + 1) * KT)
            for k in range(KT):
                if k >= 4:
                    pe.wait_ge(out_staged, k - 3)
                for t in range(TT):
                    ins = nc.tensor.transpose(bank[k % 4][:, tm_cols(t)], xT[:, k, tm_cols(t)], ident)
                ins.then_inc(ytm_done, 1)

        @block.scalar
        def _(act):
            act.wait_ge(const_loaded, 48)
            nc.scalar.copy(tri_r[:], cst[:, CONST["upper"][0]:CONST["lower"][1]].rearrange("p (s n) -> p s n", s=2))\
                .then_inc(tri_ready, 1)
            for n, name in enumerate(("ident", "mask1", "mask2")):
                nc.scalar.copy(mask_r[:, n, :], const(name)).then_inc(tri_ready, 1)
            act.wait_ge(ctrans, 1)
            nc.scalar.activation(csil[:].rearrange("p v k -> p (v k)"), aux[:, 0:16], ACT.Silu).then_inc(csil_ready, 1)
            act.wait_ge(csil_ready, 1)
            act.wait_ge(c4_ready, 1)
            nc.scalar.copy(c4[:].rearrange("p (k f) -> p k f", f=60)[:, :, 28:30], csil[:].rearrange("p v k -> p k v"))\
                .then_inc(chi_ready, 1)

            with act.Fori(0, DEPTH) as l:
                split = [0]

                def weights_to(u_end, q=None):
                    while split[0] < min(u_end, UNITS):
                        u = split[0]
                        loads, free = l * RAW_LOADS[u % RAW] * 16 + raw_count(u) * 16, l * STEPS + unit_end(u - WS)
                        if q is not None:
                            loads, free = loads + q * (Q_UNITS // RAW) * 16, free + q * Q_STEPS
                        act.wait_ge(raw_loaded[u % RAW], loads)
                        act.wait_ge(gemm_step, free)
                        if UNIT0["kvd"] <= u < UNIT0["q"]:
                            src = raw[u % RAW].rearrange("p (k n) -> p k n", k=2)[:, :, 0:KVD_COLS]
                            dst = whi[:, u % WS, :].rearrange("p (k n) -> p k n", k=2)[:, :, 0:KVD_COLS]
                        else:
                            src, dst = raw[u % RAW], whi[:, u % WS, :]
                        nc.scalar.copy(dst, src).then_inc(hi_ready, 1)
                        split[0] += 1

                def ahead(name, i):
                    weights_to(UNIT0[name] + i + WS)

                def done(name, i, m=None):
                    act.wait_ge(gemm_step, l * STEPS + step_end(name, i, m))

                def release(b, signal, value):
                    act.wait_ge(signal, value)
                    act.sem_inc(bank_free[b], 1)

                def squares(norm, k):
                    if norm == 0:
                        act.wait_ge(x_mlp, l * 4 * KT + k + 1)
                    else:
                        act.wait_ge(x_wo, l * KT + k + 1)
                    if k >= 2:
                        act.wait_ge(sq_used, (l * 2 + norm) * KT + k - 1)
                    nc.scalar.activation(tb[:, k % 2, 0:T], xT[:, k, :], ACT.Square).then_inc(sq_ready, 1)

                def h_rows(norm):
                    for k in range(KT):
                        act.wait_ge(t_ready, (l * 2 + norm) * KT + k + 1)
                        for v, (a, b) in enumerate(SEG):
                            ins = nc.scalar.activation(ahi[k][:, a:b], tb[:, 2 + k % 2, a:b], ACT.Identity,
                                                       bias=modc[:, 24 * norm + k, v:v + 1], scale=coef[:, norm, k, v:v + 1])
                        ins.then_inc(h_hi, 1)

                def mod_rows(name, part):
                    done(name, (15, 31)[part])
                    if part == 1:
                        act.wait_ge(pooled_ready, l * 4 + 4)
                    rows = (16, 32)[part]
                    nc.scalar.copy(modrow[0:rows, :], bank[0][0:rows, :]).then_inc(modrow_ready, 1)
                    release(0, modrow_ready, l * 2 + part + 1)

                def root(norm):
                    act.wait_ge(sq_used, (l * 2 + norm + 1) * KT)
                    nc.scalar.activation(tb[:, 0, 0:T], ybank[:, 0:T], ACT.Sqrt, bias=eps, scale=1.0 / D).then_inc(root_ready, 1)

                squares(0, 0)
                squares(0, 1)
                weights_to(4)
                act.wait_ge(ptrans, l + 1)
                nc.scalar.copy(pcol[:], aux[:, 0:148]).then_inc(pcol_ready, 1)
                for k in range(2, KT):
                    squares(0, k)
                    weights_to(k + 4)
                root(0)
                ahead("mod1", 15)
                mod_rows("mod1", 0)
                weights_to(UNIT0["kvd"] + 4)
                h_rows(0)
                ahead("kvd", 3)
                for t in range(TT):
                    done("kvd", 3, t)
                    nc.scalar.copy(qkv[:, t, 512:768], bank[t][:, 0:256]).then_inc(qkv_ready, 1)
                    nc.scalar.copy(dtr[:, t * 32:t * 32 + 32], bank[t][:, 256:KVD_COLS]).then_inc(bank_free[t], 1)
                ahead("q", 3)
                for t in range(TT):
                    done("q", 3, t)
                    nc.scalar.copy(qkv[:, t, 0:512], bank[t][:]).then_inc(qkv_ready, 1)
                    release(t, qkv_ready, l * 6 + 3 + t + 1)

                def conv_in(b):
                    ahead("xbc", 2 * b + 1)
                    for m in range(2):
                        j = 2 * b + m
                        done("xbc", 2 * b + 1, m)
                        if j >= 2:
                            act.wait_ge(conv_ready, l * 12 + j - 1)
                        src = bank[2 * (b % 2) + m]
                        nc.scalar.copy(cpad[:, j % 2, 2:2 + CTX], src[:, 0:CTX])
                        nc.scalar.copy(cpad[:, j % 2, 4 + CTX:4 + T], src[:, CTX:T]).then_inc(cpad_ready, 1)
                        release(2 * (b % 2) + m, cpad_ready, l * 12 + j + 1)

                def conv_out(b):
                    for j in (2 * b, 2 * b + 1):
                        act.wait_ge(conv_ready, l * 12 + j + 1)
                        dst = tb[:, 2 + j % 2, 0:CVW] if j < 8 else bc_cm[:, j - 8, :]
                        nc.scalar.activation(dst, tb[:, 2 + j % 2, 0:CVW], ACT.Silu).then_inc(silu_ready, 1)

                def x_copies(b):
                    for j in (2 * b, 2 * b + 1):
                        act.wait_ge(xtm_done, l * 10 + j + 1)
                        src = seg_ps[:, j % 2, 0:T].rearrange("p (t n) -> p t n", t=TT)
                        dst = xbuf[:, :, tm_cols(j)] if j < 8 else b_tm[:, :, tm_cols(j - 8)]
                        nc.scalar.copy(dst, src).then_inc(xtm_ready, 1)

                act.wait_ge(pads_zeroed, (l + 1) * 6)
                for b in range(6):
                    conv_in(b)
                    if b:
                        x_copies(b - 1)
                    conv_out(b)
                    if b == 0:
                        act.wait_ge(qkss_ready, l + 1)
                        nc.scalar.activation(rsq, ssq, ACT.Sqrt, bias=eps, scale=1.0 / HD).then_inc(qkroot_ready, 1)
                for b in range(2):
                    ahead("pool", 2 * b + 1)
                    for m in range(2):
                        done("pool", 2 * b + 1, m)
                        src, g = bank[2 * b + m], 2 * b + m
                        nc.scalar.copy(pu[:, g, 8:8 + CTX], src[:, 0:CTX])
                        nc.scalar.copy(pu[:, g, 16 + CTX:16 + T], src[:, CTX:T]).then_inc(pu_ready, 1)
                        release(g, pu_ready, l * 4 + g + 1)
                ahead("mod2", 4)
                act.wait_ge(dt_step, l * 5 + 2)
                nc.scalar.activation(dte, dta, ACT.Exp, scale=-1.0).then_inc(dt_act, 1)
                nc.scalar.activation(dtf[:, 0:32], alog, ACT.Exp).then_inc(dt_act, 1)
                act.wait_ge(dt_step, l * 5 + 3)
                nc.scalar.activation(dtl, dtw, ACT.Ln).then_inc(dt_act, 1)
                act.wait_ge(dt_step, l * 5 + 5)
                nc.scalar.copy(adt_hi[:], adt).then_inc(dt_act, 1)

                ahead("mod2", 8)
                act.wait_ge(qkrot_ready, l + 1)
                act.wait_ge(param_loaded, (l + 1) * 16 * 16)
                for n, src in enumerate((qkv[:, 1, 512:640], qkv[:, 2, 512:640], kvc[:, 0, :], qkv[:, 0, 512:640])):
                    nc.scalar.copy(kdup[:, n, :].rearrange("p (h a d) -> p h a d", h=2, a=2),
                                          src.rearrange("p (h d) -> p h d", h=2).unsqueeze(2).to_broadcast([P, 2, 2, 64]))\
                        .then_inc(kdup_ready, 1)

                for t in range(TT):
                    act.wait_ge(qkT_done, l * 5 + t + 1)
                    nc.scalar.copy(qT[:, :, tm_cols(t)], seg_ps[:, 0, :].rearrange("p (h t) -> p h t", h=4)).then_inc(qkT_ready, 1)
                for kv in range(2):
                    act.wait_ge(qkT_done, l * 5 + 4 + kv)
                    nc.scalar.copy(kT[:, kv, :], seg_ps[:, 1, :]).then_inc(qkT_ready, 1)

                def prob_exp(i):
                    t = i // 4
                    n = P if t == 0 else 3 * P
                    act.wait_ge(nbias_ready, l * 12 + i + 1)
                    if i:
                        act.wait_ge(pT_done, l * 12 + i)
                    for h in range(2):
                        nc.scalar.activation(prob[:, h, 0:n], seg_ps[:, h, 0:n], ACT.Exp, bias=nbias[:, h:h + 1], scale=SCALE,
                                             accum_out=den[:, h:h + 1]).then_inc(probs_exp, 1)
                    act.wait_ge(sadd_ready, l * 12 + i + 1)
                    nc.scalar.activation(sexp, sadd, ACT.Exp).then_inc(sexp_ready, 1)

                def attn_round(i):
                    t, hp = i // 4, i % 4
                    act.wait_ge(pv_done, l * 12 + i + 1)
                    nc.scalar.copy(bhi[4 + hp][:, tm_cols(t)], ybank[:, 384:512]).then_inc(attn_hi, 1)

                def pool_round(g):
                    act.wait_ge(pmix_done, l * 4 + g + 1)
                    nc.scalar.activation(bhi[g][:, :], bank[POOL_BANK[g]][:, 0:T], ACT.Copy, scale=pscol[:, g:g + 1])\
                        .then_inc(pmix_hi, 1)

                prob_exp(0)
                for i in range(12):
                    n = 1 if i < 4 else 3
                    act.wait_ge(pT_done, l * 12 + i + 1)
                    nc.scalar.copy(probT[:, :, 0:n * P], y_ps[:, :, 0:n * P]).then_inc(pT_ready, 1)
                    if i < 11:
                        prob_exp(i + 1)
                    attn_round(i)
                    ahead("mod2", 10 + 2 * i)
                    if i >= 9:
                        pool_round(i - 9)
                mod_rows("mod2", 1)
                pool_round(3)
                act.wait_ge(cum_done, l + 1)
                nc.scalar.copy(acs, aux[:, 0:96]).then_inc(acs_ready, 1)
                nc.scalar.activation(eac, aux[:, 0:96], ACT.Exp).then_inc(acs_ready, 1)
                nc.scalar.activation(etot, aux[:, 96:192], ACT.Exp).then_inc(acs_ready, 1)
                act.wait_ge(rem_ready, l + 1)
                nc.scalar.activation(wdec, dtm, ACT.Exp).then_inc(decay_ready, 1)

                gates = {"gpa": 0, "gpb": 1, "gaa": 2, "gab": 3, "gsa": 4, "gsb": 5}
                filler = [(n, i) for n, k, _ in STAGES[6:16] for i in range(k)]
                filled = [0]

                def fill(n=1):
                    for _ in range(n):
                        name, i = filler[filled[0]]
                        filled[0] += 1
                        ahead(name, i)
                        if name not in gates or i % 2 == 0:
                            continue
                        b = i // 2
                        for m in range(2):
                            at = gates[name] * 4 + 2 * b + m
                            done(name, i, m)
                            if name == "gsb":
                                dst = gate2[2 * b + m]
                            else:
                                dst = gate[2 * b + m]
                                if at >= 4:
                                    act.wait_ge(gated_ready, l * 24 + at - 3)
                            if at == 0:
                                act.wait_ge(attn_ready, l * 12 + 12)
                                act.wait_ge(kv_out, (l + 1) * 32)
                            nc.scalar.activation(dst, bank[2 * (b % 2) + m][:, 0:T], ACT.Tanh, scale=0.5)\
                                .then_inc(gate_ready, 1)
                            release(2 * (b % 2) + m, gate_ready, l * 24 + at + 1)

                def seg_exp(g, i):
                    act.wait_ge(seg_done, (l * 2 + g) * 6 + i + 1)
                    if i >= 2 or g:
                        act.wait_ge(ydiag_done, (l * 2 + g) * 6 + i - 1)
                    nc.scalar.activation(ew[:, i % 2].rearrange("p h i -> p (h i)"), seg_ps[:].rearrange("p b n -> p (b n)"),
                                         ACT.Exp).then_inc(exp_ready, 1)

                def evac(g, n, dst, signal):
                    act.wait_ge(aux_done, (l * 2 + g) * 13 + n + 1)
                    nc.scalar.copy(dst, aux).then_inc(signal, 1)
                    return signal

                for g in range(2):
                    def keep(n, dst, signal, value):
                        evac(g, n, dst, signal)
                        act.wait_ge(signal, value)
                        act.sem_inc(aux_free, 1)

                    seg_exp(g, 0)
                    fill()
                    keep(1, st[:, 0, :], st_ready, (l * 2 + g) * 2 + 1)
                    seg_exp(g, 1)
                    fill()
                    keep(2, st[:, 1, :], st_ready, (l * 2 + g) * 2 + 2)
                    seg_exp(g, 2)
                    fill()
                    fill()
                    seg_exp(g, 3)
                    fill()
                    keep(5, stage[:, 0, :], stT_ready, (l * 2 + g) * 2 + 1)
                    fill(2)
                    keep(6, stage[:, 1, :], state_staged, (l * 2 + g) * 2 + 1)
                    seg_exp(g, 4)
                    fill()
                    keep(7, stage[:, 0, :], stT_ready, (l * 2 + g) * 2 + 2)
                    fill(2)
                    keep(8, stage[:, 2, :], state_staged, (l * 2 + g) * 2 + 2)
                    seg_exp(g, 5)
                    fill(6)

                for n in range(2):
                    ahead("z", 4 * n + 3)
                    for t in range(TT):
                        i = 3 * n + t
                        done("z", 4 * n + 3, t)
                        if i >= 2:
                            act.wait_ge(yz_ready, l * 6 + i - 1)
                        else:
                            act.wait_ge(ydiag_done, (l + 1) * 12)
                        nc.scalar.activation(dtx[:, i % 2, :], bank[t][:], ACT.Silu).then_inc(zs_ready, 1)
                        release(t, zs_ready, l * 6 + i + 1)
                for t in range(TT):
                    if t == 2:
                        act.wait_ge(ysq_ready, l * TT + 1)
                    act.wait_ge(yz_ready, l * 6 + 4 + t)
                    nc.scalar.activation(ew[:, t % 2].rearrange("p h i -> p (h i)"), xbuf[:, t, :], ACT.Square,
                                         accum_out=ysum[:, t:t + 1]).then_inc(ysq_ready, 1)
                act.wait_ge(ysq_ready, (l + 1) * TT)
                nc.scalar.activation(yrs, ysum, ACT.Sqrt, bias=eps, scale=1.0 / INNER).then_inc(yroot_ready, 1)
                for k in range(KT):
                    act.wait_ge(ytrans, l * KT + k + 1)
                    spare = (seg_ps[:, 0, :], seg_ps[:, 1, :], ybank, aux)[k % 4]
                    nc.scalar.activation(ahi[k][:, :], spare[:, 0:T], ACT.Copy, scale=ssdcol[:, k:k + 1]).then_inc(ssd_hi, 1)
                for b in range(4):
                    ahead("so", 2 * b + 1)
                    for m in range(2):
                        act.wait_ge(merged_full, l * KT + 2 * b + m + 1)
                        nc.scalar.activation(bhi[2 * b + m][:, :], merged[:, 2 * b + m, :], ACT.Copy, scale=0.5).then_inc(m_hi, 1)
                for b in range(4):
                    ahead("wo", 2 * b + 1)
                    for m in range(2):
                        squares(1, 2 * b + m)
                root(1)
                weights_to(UNIT0["mlp"] + WS)
                h_rows(1)

                def mlp_quarter(q, j_last):
                    split[0] = UNIT0["mlp"] + WS

                    def weights(i):
                        weights_to(UNIT0["mlp"] + min(i + WS, j_last), q)

                    for b in range(4):
                        weights(2 * b + 1)
                        for m in range(2):
                            k = 2 * b + m
                            act.wait_ge(gemm_step, l * STEPS + step_end("mlp", 2 * b + 1, m) + q * Q_STEPS)
                            act.wait_ge(hid_ready, (l * 4 + q) * KT + HID_PRIME + k - 1)
                            nc.scalar.activation(tb[:, k % 2, 0:T], bank[2 * (b % 2) + m][:, 0:T], ACT.Relu).then_inc(relu_ready, 1)
                            release(2 * (b % 2) + m, relu_ready, (l * 4 + q) * KT + k + 1)
                            nc.scalar.activation(bhi[k][:, :], tb[:, k % 2, 0:T], ACT.Square).then_inc(hid_hi, 1)
                    for i in range(9, 16, 2):
                        weights(i)
                    weights(Q_UNITS)

                with act.Fori(0, 3) as q:
                    mlp_quarter(q, Q_UNITS + WS)
                mlp_quarter(3, Q_UNITS)

            for k in range(KT):
                act.wait_ge(ytm_done, k + 1)
                nc.scalar.copy(xbuf[:, :, tm_cols(k)], bank[k % 4][:, 0:T].rearrange("p (t n) -> p t n", t=TT))\
                    .then_inc(out_staged, 1)

        @block.vector
        def _(dve):
            for b in range(4):
                dve.sem_inc(bank_free[b], 1)
            dve.sem_inc(hid_ready, HID_PRIME)
            dve.sem_inc(ssd_ready, 1)
            nc.vector.memset(c4[:].bitcast(F32), 0.0).then_inc(c4_ready, 1)
            for k in range(KT):
                dve.wait_ge(xtrans, k + 1)
                nc.vector.tensor_copy(xT[:, k, :], bank[k % 4][:, 0:T]).then_inc(x_mlp, 1)
            dve.wait_ge(chi_ready, 1)
            c4f = c4[:].rearrange("p (k f) -> p k f", f=60)
            nc.vector.tensor_tensor(c4f[:, :, 30:32], csil[:].rearrange("p v k -> p k v"), c4f[:, :, 28:30].bitcast(F32),
                                    ALU.subtract).then_inc(c4_ready, 1)

            with dve.Fori(0, DEPTH) as l:
                split, linked = [0], [0]

                def link(ins):
                    linked[0] += 1
                    ins.then_inc(dve_link, 1)
                    dve.wait_ge(dve_link, l * DVE_LINKS + linked[0])

                def weights_to(u_end, q=None):
                    while split[0] < min(u_end, UNITS):
                        u = split[0]
                        value = l * UNITS + u + 1
                        dve.wait_ge(hi_ready, value if q is None else value + q * Q_UNITS)
                        full, top, rest = raw[u % RAW], whi[:, u % WS, :], wlo[u % RAW]
                        if UNIT0["kvd"] <= u < UNIT0["q"]:
                            full, top, rest = (w.rearrange("p (k n) -> p k n", k=2)[:, :, 0:KVD_COLS] for w in (full, top, rest))
                        nc.vector.tensor_tensor(rest, full, top.bitcast(F32), ALU.subtract).then_inc(lo_ready, 1)
                        split[0] += 1

                def ahead(name, i):
                    weights_to(UNIT0[name] + i + WS)

                def done(name, i, m=None):
                    dve.wait_ge(gemm_step, l * STEPS + step_end(name, i, m))

                def release(b, signal, value):
                    dve.wait_ge(signal, value)
                    dve.sem_inc(bank_free[b], 1)

                def norm_rows(norm):
                    rstd = tb[:, 0, 0:T]
                    dve.wait_ge(root_ready, l * 2 + norm + 1)
                    link(nc.vector.reciprocal(rstd, rstd))

                    def scaled(k):
                        nc.vector.tensor_tensor(tb[:, 2 + k % 2, 0:T], xT[:, k, :], rstd, ALU.mult).then_inc(t_ready, 1)

                    scaled(0)
                    scaled(1)
                    for k in range(KT):
                        dve.wait_ge(h_hi, (l * 2 + norm) * KT + k + 1)
                        row = tb[:, 2 + k % 2, :]
                        for v, (a, b) in enumerate(SEG):
                            ins = nc.vector.tensor_scalar(row[:, a:b], row[:, a:b], coef[:, norm, k, v:v + 1],
                                                          modc[:, 24 * norm + k, v:v + 1], ALU.mult, ALU.add)
                        link(ins)
                        nc.vector.tensor_tensor(alo[k][:, :], row[:, 0:T], ahi[k][:, :].bitcast(F32), ALU.subtract)\
                            .then_inc(h_ready, 1)
                        if k + 2 < KT:
                            dve.wait_ge(h_ready, (l * 2 + norm) * KT + k + 1)
                            scaled(k + 2)

                def modulation(part):
                    a, b = ((0, 16), (16, 48))[part]
                    n, at = ((4, 384), (8, 416))[part]
                    dve.wait_ge(modcol_done, l * 2 + part + 1)
                    if part == 0:
                        dve.wait_ge(pcol_ready, l + 1)
                    nc.vector.tensor_tensor(modc[:, a:b, :].rearrange("p (n j) v -> p n j v", j=4),
                                            aux[:, at:at + 8 * n].rearrange("p (j n v) -> p n j v", j=4, v=2),
                                            bmcol[:, a:b].rearrange("p (n j) -> p n j", j=4).unsqueeze(3)
                                            .to_broadcast([P, n, 4, 2]), ALU.add)\
                        .then_inc(modc_ready, 1)
                    dve.wait_ge(modc_ready, l * 2 + part + 1)
                    gain = (n1col, n2col)[part]
                    s = (8, 32)[part]
                    link(nc.vector.scalar_tensor_tensor(coef[:, part], modc[:, s:s + 8, :], 1.0,
                                                        gain.unsqueeze(2).to_broadcast([P, KT, 2]), ALU.add, ALU.mult))

                dve.wait_ge(ssd_ready, l * KT + 1)
                dve.wait_ge(state_out, l * 64 + 1)
                for a, b in ((0, 2), (2 + CTX, 4 + CTX), (4 + T, 6 + T)):
                    nc.vector.memset(cpad[:, :, a:b], 0.0).then_inc(pads_zeroed, 1)
                for a, b in ((0, 8), (8 + CTX, 16 + CTX), (16 + T, 24 + T)):
                    nc.vector.memset(pu[:, :, a:b], 0.0).then_inc(pads_zeroed, 1)

                ahead("mod1", 15)
                dve.wait_ge(param_loaded, (l + 1) * 16 * 16)
                link(nc.vector.tensor_scalar(nsink, sink, -1.0, None, ALU.mult))
                modulation(0)
                norm_rows(0)
                ahead("kvd", 3)
                ahead("q", 3)

                def conv(b):
                    ahead("xbc", 2 * b + 1)
                    for j in (2 * b, 2 * b + 1):
                        dve.wait_ge(cpad_ready, l * 12 + j + 1)
                        if 2 <= j < 10:
                            dve.wait_ge(xtm_done, l * 10 + j - 1)
                        elif j >= 10:
                            dve.wait_ge(silu_ready, l * 12 + j - 1)
                        row, src = tb[:, 2 + j % 2, 0:CVW], cpad[:, j % 2, :]
                        link(nc.vector.tensor_scalar(row, src[:, 0:CVW], convw[:, 0, j:j + 1], convb[:, j:j + 1], ALU.mult, ALU.add))
                        for w in range(1, CONV_W):
                            ins = nc.vector.scalar_tensor_tensor(row, src[:, w:w + CVW], convw[:, w, j:j + 1], row, ALU.mult, ALU.add)
                            if w < CONV_W - 1:
                                link(ins)
                        ins.then_inc(conv_ready, 1)

                def qk_norm():
                    dve.wait_ge(qksq_ready, l + 1)
                    heads = [P, TT, NQK, HD]
                    nc.vector.tensor_reduce(ssq, rtmp.rearrange("p t (h d) -> p t h d", d=HD), AX_X, ALU.add).then_inc(qkss_ready, 1)
                    dve.wait_ge(qkroot_ready, l + 1)
                    link(nc.vector.reciprocal(rsq, rsq))
                    qk = qkv[:, :, 0:640].rearrange("p t (h d) -> p t h d", d=HD)
                    for t in range(TT):
                        link(nc.vector.tensor_tensor(qk[:, t], qk[:, t], rsq[:, 10 * t:10 * t + 10].unsqueeze(2)
                                                     .to_broadcast([P, NQK, HD]), ALU.mult))
                    for t in range(TT):
                        nc.vector.tensor_tensor(qk[:, t, 0:8], qk[:, t, 0:8], qg.unsqueeze(1).to_broadcast([P, 8, HD]), ALU.mult)
                        ins = nc.vector.tensor_tensor(qk[:, t, 8:10], qk[:, t, 8:10], kg.unsqueeze(1).to_broadcast([P, 2, HD]),
                                                      ALU.mult)
                    ins.then_inc(qkn_ready, 1)
                    dve.wait_ge(qkn_ready, l + 1)

                def qk_rope():
                    qk = qkv[:, :, 0:640].rearrange("p t (h d) -> p t h d", d=HD)
                    rt = rtmp.rearrange("p t (h d) -> p t h d", d=HD)
                    for t in (1, 2):
                        link(nc.vector.tensor_tensor(rt[:, 0], qk[:, t], rope[:, t - 1, 0:1, :].to_broadcast([P, NQK, HD]), ALU.mult))
                        dve.wait_ge(qkrot_half, l * 4 + 2 * t)
                        ins = nc.vector.tensor_tensor(qk[:, t], rt[:, 0], rt[:, t], ALU.add)
                        if t == 1:
                            link(ins)
                    ins.then_inc(qkrot_ready, 1)

                def softplus():
                    by_t = lambda v: v.rearrange("p (t h) -> p t h", t=TT)
                    wide = lambda v: v.unsqueeze(1).to_broadcast([P, TT, 2 * SH])
                    nc.vector.tensor_tensor(by_t(dtv), by_t(dtr), wide(dtb), ALU.add).then_inc(dt_step, 1)
                    dve.wait_ge(dt_step, l * 5 + 1)
                    nc.vector.scalar_tensor_tensor(dta, dtv, -1.0, dtv, ALU.mult, ALU.max).then_inc(dt_step, 1)
                    dve.wait_ge(dt_act, l * 4 + 1)
                    nc.vector.tensor_scalar(dtw, dte, 1.0, None, ALU.add).then_inc(dt_step, 1)
                    dve.wait_ge(dt_step, l * 5 + 3)
                    link(nc.vector.tensor_scalar(dtm, dtw, 1.0, None, ALU.is_equal))
                    link(nc.vector.scalar_tensor_tensor(dtd, dtw, -1.0, dtm, ALU.add, ALU.add))
                    link(nc.vector.reciprocal(dtd, dtd))
                    dve.wait_ge(dt_act, l * 4 + 3)
                    link(nc.vector.tensor_tensor(dtl, dtl, dtd, ALU.mult))
                    link(nc.vector.tensor_tensor(dtl, dtl, dtm, ALU.add))
                    link(nc.vector.tensor_tensor(dtl, dtl, dte, ALU.mult))
                    nc.vector.scalar_tensor_tensor(dta, dtv, 0.0, dtl, ALU.max, ALU.add).then_inc(dt_step, 1)
                    dve.wait_ge(dt_step, l * 5 + 4)
                    nc.vector.scalar_tensor_tensor(by_t(adt), by_t(dta), -1.0, wide(dtf[:, 0:32]), ALU.mult, ALU.mult)\
                        .then_inc(dt_step, 1)
                    dve.wait_ge(dt_act, l * 4 + 4)
                    link(nc.vector.tensor_tensor(adt_lo[:], adt, adt_hi[:].bitcast(F32), ALU.subtract))
                    nc.vector.tensor_scalar(nadt_hi[:], adt_hi[:].bitcast(F32), -1.0, None, ALU.mult)
                    nc.vector.tensor_scalar(nadt_lo[:], adt_lo[:].bitcast(F32), -1.0, None, ALU.mult).then_inc(adt_ready, 1)

                conv(0)
                qk_norm()
                conv(1)
                qk_rope()
                for b in range(2, 6):
                    conv(b)
                ahead("mod2", 4)
                softplus()
                ahead("mod2", 8)

                def head_max(i):
                    t, hp = i // 4, i % 4
                    n = P if t == 0 else 3 * P
                    dve.wait_ge(scores_ready, l * 12 + i + 1)
                    link(nc.vector.tensor_reduce(nmax, seg_ps[:, :, 0:n], AX_X, ALU.max, negate=True))
                    nc.vector.scalar_tensor_tensor(nbias, nmax, SCALE, nsink[:, 2 * hp:2 * hp + 2], ALU.mult, ALU.min)\
                        .then_inc(nbias_ready, 1)
                    dve.wait_ge(nbias_ready, l * 12 + i + 1)
                    nc.vector.tensor_tensor(sadd, nbias, sink[:, 2 * hp:2 * hp + 2], ALU.add).then_inc(sadd_ready, 1)

                def head_norm(i):
                    n = P if i < 4 else 3 * P
                    dve.wait_ge(sexp_ready, l * 12 + i + 1)
                    link(nc.vector.tensor_tensor(den, den, sexp, ALU.add))
                    link(nc.vector.reciprocal(rden, den))
                    for h in range(2):
                        ins = nc.vector.tensor_scalar(prob[:, h, 0:n], prob[:, h, 0:n], rden[:, h:h + 1], None, ALU.mult)
                    ins.then_inc(probs_ready, 1)

                def attn_rest(i):
                    t, hp = i // 4, i % 4
                    dve.wait_ge(attn_hi, l * 12 + i + 1)
                    nc.vector.tensor_tensor(blo[4 + hp][:, tm_cols(t)], ybank[:, 384:512], bhi[4 + hp][:, tm_cols(t)].bitcast(F32),
                                            ALU.subtract).then_inc(attn_ready, 1)

                def pooled(g):
                    dve.wait_ge(pwin_ready, l * 4 + g + 1)
                    a, b = 8, 16 + T
                    nc.vector.scalar_tensor_tensor(pu[:, g, a:b], pwin[:, g % 2, a:b], 1.0 / WINDOWS[g], pu[:, g, a:b],
                                                   ALU.mult, ALU.subtract).then_inc(pooled_ready, 1)

                def pool_rest(g):
                    b = POOL_BANK[g]
                    dve.wait_ge(pmix_hi, l * 4 + g + 1)
                    nc.vector.scalar_tensor_tensor(blo[g][:, :], bank[b][:, 0:T], pscol[:, g:g + 1], bhi[g][:, :].bitcast(F32),
                                                   ALU.mult, ALU.subtract).then_inc(pmix_ready, 1)
                    release(b, pmix_ready, l * 4 + g + 1)

                head_max(0)
                for i in range(12):
                    head_norm(i)
                    if i:
                        ahead("mod2", 8 + 2 * i)
                    if i < 11:
                        head_max(i + 1)
                    ahead("mod2", 9 + 2 * i)
                    attn_rest(i)
                    if i in (1, 3, 5, 7):
                        pooled(i // 2)
                    if i >= 10:
                        pool_rest(i - 10)
                ahead("mod2", 32)
                pool_rest(2)
                pool_rest(3)
                modulation(1)
                dve.wait_ge(acs_ready, l * 3 + 3)
                nc.vector.tensor_tensor(dtm, aux[:, 96:192], acs, ALU.subtract).then_inc(rem_ready, 1)
                dve.wait_ge(decay_ready, l + 1)
                nc.vector.tensor_tensor(wdec, wdec, dta, ALU.mult).then_inc(wdec_ready, 1)

                filler = [(n, i) for n, k, _ in STAGES[6:16] for i in range(k)]
                filled = [0]

                def gated(k, at, psum, dst, gates):
                    dve.wait_ge(gate_ready, l * 24 + at + 1)
                    nc.vector.scalar_tensor_tensor(dst, gates[k % 4], 1.0, psum[:, 0:T], ALU.add, ALU.mult)\
                        .then_inc(gated_ready, 1)

                def fill(n=1):
                    for _ in range(n):
                        name, i = filler[filled[0]]
                        filled[0] += 1
                        ahead(name, i)
                        if name not in ("poa", "pob", "aoa", "aob"):
                            continue
                        half, attn = name[2] == "b", name[0] == "a"
                        for m in range(2):
                            k = 4 * half + 2 * i + m
                            at = 8 * attn + k
                            done(name, i, m)
                            dst = mtmp if attn else merged[:, k, :]
                            gated(k, at, bank[2 * (i % 2) + m], dst, gate)
                            release(2 * (i % 2) + m, gated_ready, l * 24 + at + 1)
                            if attn:
                                link(nc.vector.tensor_tensor(merged[:, k, :], merged[:, k, :], mtmp, ALU.add))

                def weigh(g, i):
                    t, e = i // 2, i % 2
                    dve.wait_ge(exp_ready, (l * 2 + g) * 6 + i + 1)
                    nc.vector.scalar_tensor_tensor(ew[:, e], ew[:, e], 1.0, cbs[:, t, :].unsqueeze(1).to_broadcast([P, HG, P]),
                                                   ALU.min, ALU.mult).then_inc(w_ready, 1)

                def per_head(values, t, e, g):
                    a = t * 32 + e * 16 + g * 8
                    return values[:, a:a + 8].unsqueeze(2).to_broadcast([P, HG, HD])

                def heads(rows):
                    return rows.rearrange("p (h d) -> p h d", d=HD)

                def next_state(g, n, t, e, src, dst):
                    dve.wait_ge(st_ready, (l * 2 + g) * 2 + src + 1)
                    link(nc.vector.tensor_tensor(heads(st[:, dst, :]), heads(st[:, src, :]), per_head(etot, t, e, g), ALU.mult))
                    dve.wait_ge(aux_done, (l * 2 + g) * 13 + n + 1)
                    nc.vector.tensor_tensor(st[:, dst, :], st[:, dst, :], aux, ALU.add).then_inc(aux_free, 1)

                def y_diag(g, t):
                    cols = slice(g * 512, g * 512 + 512)
                    dve.wait_ge(xd_ready, (l * 2 + g) * 3 + t + 1)
                    dve.wait_ge(ydiag_done, (l * 2 + g) * 6 + 2 * t + 2)
                    nc.vector.tensor_tensor(xbuf[:, t, cols], xbuf[:, t, cols], ybank, ALU.add).then_inc(y_free, 1)
                    dve.wait_ge(y_free, (l * 2 + g) * 3 + t + 1)

                def y_off(g, n, t, e):
                    cols = slice(g * 512, g * 512 + 512)
                    dve.wait_ge(aux_done, (l * 2 + g) * 13 + n + 1)
                    nc.vector.tensor_tensor(heads(ytmp), heads(aux), per_head(eac, t, e, g), ALU.mult).then_inc(aux_free, 1)
                    dve.wait_ge(aux_free, (l * 2 + g) * 13 + n + 1)
                    link(nc.vector.tensor_tensor(xbuf[:, t, cols], xbuf[:, t, cols], ytmp, ALU.add))

                for g in range(2):
                    dve.wait_ge(aux_done, (l * 2 + g) * 13 + 1)
                    if g:
                        dve.wait_ge(w_ready, (l * 2 + g) * 6)
                    nc.vector.tensor_copy(cbs[:].rearrange("p t n -> p (t n)"), aux[:, 0:T]).then_inc(aux_free, 1)
                    dve.wait_ge(aux_free, (l * 2 + g) * 13 + 1)
                    weigh(g, 0)
                    fill()
                    weigh(g, 1)
                    fill()
                    weigh(g, 2)
                    fill()
                    next_state(g, 3, 2, 1, 1, 3)
                    fill()
                    next_state(g, 4, 1, 0, 0, 2)
                    weigh(g, 3)
                    y_diag(g, 0)
                    fill(3)
                    weigh(g, 4)
                    fill()
                    y_diag(g, 1)
                    fill(2)
                    weigh(g, 5)
                    fill()
                    y_off(g, 9, 1, 0)
                    fill()
                    y_off(g, 10, 1, 1)
                    fill()
                    y_diag(g, 2)
                    y_off(g, 11, 2, 0)
                    fill()
                    y_off(g, 12, 2, 1)
                    fill(2)

                for n in range(2):
                    ahead("z", 4 * n + 3)
                    for t in range(TT):
                        cols = slice(n * 512, n * 512 + 512)
                        dve.wait_ge(zs_ready, l * 6 + 3 * n + t + 1)
                        nc.vector.tensor_tensor(xbuf[:, t, cols], xbuf[:, t, cols], dtx[:, (3 * n + t) % 2, :], ALU.mult)\
                            .then_inc(yz_ready, 1)
                dve.wait_ge(yroot_ready, l + 1)
                link(nc.vector.reciprocal(yrs, yrs))
                for t in range(TT):
                    nc.vector.tensor_scalar(xbuf[:, t, :], xbuf[:, t, :], yrs[:, t:t + 1], None, ALU.mult).then_inc(yn_ready, 1)
                for k in range(KT):
                    dve.wait_ge(ssd_hi, l * KT + k + 1)
                    spare = (seg_ps[:, 0, :], seg_ps[:, 1, :], ybank, aux)[k % 4]
                    nc.vector.scalar_tensor_tensor(alo[k][:, :], spare[:, 0:T], ssdcol[:, k:k + 1], ahi[k][:, :].bitcast(F32),
                                                   ALU.mult, ALU.subtract).then_inc(ssd_ready, 1)
                for b in range(4):
                    ahead("so", 2 * b + 1)
                    for m in range(2):
                        k = 2 * b + m
                        done("so", 2 * b + 1, m)
                        gated(k, 16 + k, bank[2 * (b % 2) + m], mtmp, gate if k < 4 else gate2)
                        release(2 * (b % 2) + m, gated_ready, l * 24 + 16 + k + 1)
                        nc.vector.tensor_tensor(merged[:, k, :], merged[:, k, :], mtmp, ALU.add).then_inc(merged_full, 1)
                        dve.wait_ge(m_hi, l * KT + k + 1)
                        nc.vector.scalar_tensor_tensor(blo[k][:, :], merged[:, k, :], 0.5, bhi[k][:, :].bitcast(F32), ALU.mult,
                                                       ALU.subtract).then_inc(m_ready, 1)

                def add_to_x(k, gain, psum, signal):
                    for v, (a, b) in enumerate(SEG):
                        ins = nc.vector.scalar_tensor_tensor(xT[:, k, a:b], psum[:, a:b], modc[:, gain + k, v:v + 1], xT[:, k, a:b],
                                                             ALU.mult, ALU.add)
                    ins.then_inc(signal, 1)

                for b in range(4):
                    ahead("wo", 2 * b + 1)
                    for m in range(2):
                        k = 2 * b + m
                        done("wo", 2 * b + 1, m)
                        add_to_x(k, 16, bank[2 * (b % 2) + m], x_wo)
                        release(2 * (b % 2) + m, x_wo, l * KT + k + 1)
                weights_to(UNIT0["mlp"] + WS)
                norm_rows(1)

                def mlp_quarter(q, j_last):
                    split[0] = UNIT0["mlp"] + WS

                    def weights(i):
                        weights_to(UNIT0["mlp"] + min(i + WS, j_last), q)

                    for b in range(4):
                        weights(2 * b + 1)
                        for m in range(2):
                            k = 2 * b + m
                            row = tb[:, 2 + k % 2, 0:T]
                            dve.wait_ge(relu_ready, (l * 4 + q) * KT + k + 1)
                            nc.vector.tensor_tensor(row, tb[:, k % 2, 0:T], tb[:, k % 2, 0:T], ALU.mult).then_inc(hid_sq, 1)
                            dve.wait_ge(hid_sq, (l * 4 + q) * KT + k + 1)
                            dve.wait_ge(hid_hi, (l * 4 + q) * KT + k + 1)
                            nc.vector.tensor_tensor(blo[k][:, :], row, bhi[k][:, :].bitcast(F32), ALU.subtract).then_inc(hid_ready, 1)
                    for b in range(4):
                        weights(8 + 2 * b + 1)
                        for m in range(2):
                            k = 2 * b + m
                            dve.wait_ge(gemm_step, l * STEPS + step_end("mlp", 8 + 2 * b + 1, m) + q * Q_STEPS)
                            add_to_x(k, 40, bank[2 * (b % 2) + m], x_mlp)
                            release(2 * (b % 2) + m, x_mlp, (l * 4 + q) * KT + KT + k + 1)
                    weights(Q_UNITS)

                with dve.Fori(0, 3) as q:
                    mlp_quarter(q, Q_UNITS + WS)
                mlp_quarter(3, Q_UNITS)
                assert linked[0] == DVE_LINKS, linked[0]

        @block.gpsimd
        def _(pool):
            pool.sem_inc(state_out, 1)
            with pool.Fori(0, DEPTH) as l:
                pool.wait_ge(qkv_ready, (l + 1) * 6)
                nc.gpsimd.tensor_tensor(rtmp, qkv[:, :, 0:640], qkv[:, :, 0:640], ALU.mult).then_inc(qksq_ready, 1)
                pool.wait_ge(qkn_ready, l + 1)
                for t in (1, 2):
                    x = qkv[:, t, 0:640].rearrange("p (a j i) -> p a j i", j=2, i=16)
                    dst = rtmp[:, t, :].rearrange("p (a j i) -> p a j i", j=2, i=16)
                    s = rope[:, t - 1, 1, :].rearrange("p (a j i) -> p a j i", a=2, j=2)
                    for j in range(2):
                        half = s[:, :, j, :].unsqueeze(1).to_broadcast([P, NQK, 2, 16])
                        nc.gpsimd.tensor_tensor(dst[:, :, j, :].rearrange("p (h a) i -> p h a i", a=2),
                                                x[:, :, 1 - j, :].rearrange("p (h a) i -> p h a i", a=2), half, ALU.mult)\
                            .then_inc(qkrot_half, 1)

                pool_links = [0]

                def link(ins):
                    pool_links[0] += 1
                    ins.then_inc(pool_link, 1)
                    pool.wait_ge(pool_link, l * POOL_LINKS + pool_links[0])

                for g in range(4):
                    pool.wait_ge(pu_ready, l * 4 + g + 1)
                    if g:
                        pool.wait_ge(pooled_ready, l * 4 + g)
                    u = pu[:, g, :]
                    link(nc.gpsimd.tensor_tensor(pwin[:, 0, 1:PPW], u[:, 0:PPW - 1], u[:, 1:PPW], ALU.add))
                    lo, hi, shift = 1, PPW, 1
                    for level in range(1, g + 1):
                        lo, hi = lo + shift, hi - shift
                        a, b = pwin[:, (level - 1) % 2, :], pwin[:, level % 2, :]
                        link(nc.gpsimd.tensor_tensor(b[:, lo:hi], a[:, lo - shift:hi - shift], a[:, lo + shift:hi + shift], ALU.add))
                        shift *= 2
                    s = pwin[:, g % 2, :]
                    for a, b in ((8, 8 + CTX), (16 + CTX, 16 + T)):
                        ends = s[:, a:b].rearrange("p (e i) -> p e i", i=8)[:, ::(b - a) // 8 - 1, :]
                        ins = nc.gpsimd.tensor_tensor(ends, ends, edge[:, g], ALU.mult)
                    ins.then_inc(pwin_ready, 1)

                pool.wait_ge(wdec_ready, l + 1)

                def weighted(dst, values, g, t, e):
                    a = t * 32 + e * 16 + g * 8
                    return nc.gpsimd.tensor_tensor(dst.rearrange("p (h d) -> p h d", d=HD),
                                                   xbuf[:, t, g * 512:g * 512 + 512].rearrange("p (h d) -> p h d", d=HD),
                                                   values[:, a:a + 8].unsqueeze(2).to_broadcast([P, HG, HD]), ALU.mult)

                def dtx_rows(g, t):
                    if t or g:
                        pool.wait_ge(ydiag_done, (l * 2 + g) * 6 + 2 * t)
                    weighted(dtx[:, 0, :], dta, g, t, 0)
                    weighted(dtx[:, 1, :], dta, g, t, 1).then_inc(dtx_ready, 1)

                def skip_rows(g, t):
                    pool.wait_ge(dtx_ready, (l * 2 + g) * 3 + t + 1)
                    pool.wait_ge(dtxd_ready, (l * 2 + g) * 4 + 4)
                    rows = xbuf[:, t, g * 512:g * 512 + 512].rearrange("p (h d) -> p h d", d=HD)
                    nc.gpsimd.tensor_tensor(rows, rows, dskip[:, g * 8:g * 8 + 8].unsqueeze(2).to_broadcast([P, HG, HD]), ALU.mult)\
                        .then_inc(xd_ready, 1)

                for g in range(2):
                    def to_end(buf, t, e, n):
                        if n is not None:
                            pool.wait_ge(aux_done, (l * 2 + g) * 13 + n)
                        weighted(dtxd[:, buf, :], wdec, g, t, e).then_inc(dtxd_ready, 1)

                    dtx_rows(g, 0)
                    to_end(0, 2, 1, None if g == 0 else -13 + 6)
                    to_end(1, 1, 0, None if g == 0 else -13 + 8)
                    to_end(0, 0, 0, 4)
                    to_end(1, 0, 1, 5)
                    skip_rows(g, 0)
                    dtx_rows(g, 1)
                    skip_rows(g, 1)
                    dtx_rows(g, 2)
                    skip_rows(g, 2)
                assert pool_links[0] == POOL_LINKS, pool_links[0]


_INS = ["x_prompt", "x_sample", "cache_k", "cache_v", "state_ssd", "c", "c_ctx", "w_mod", "b_mod", "norm1_g", "norm2_g",
        "w_in", "pool_w", "pool_scale", "w_pool_o", "q_norm_g", "k_norm_g", "attn_sink", "w_attn_o", "conv_w", "conv_b",
        "dt_bias", "a_log", "d_skip", "ssd_norm_g", "w_ssd_o", "w_out", "w_mlp1", "w_mlp2"]
_OUTS = [(1, CTX, D), (1, LAT, D), (1, DEPTH, CTX, NKV, HD), (1, DEPTH, CTX, NKV, HD), (1, DEPTH, 2, SH, 64, 128)]


def kernel(**inputs):
    import concourse.bacc as _bacc
    from concourse.bass_utils import run_bass_kernel_spmd as _run

    nc = _bacc.Bacc("TRN2", target_bir_lowering=False, num_devices=1)
    arrays, args = {"consts_dram": constants()}, []
    args.append(nc.dram_tensor("consts_dram", (P, CONST_COLS), F32, kind="ExternalInput").ap())
    for name in _INS:
        a = np.ascontiguousarray(inputs[name])
        arrays[f"in_{name}_dram"] = a
        args.append(nc.dram_tensor(f"in_{name}_dram", a.shape, mybir.dt.from_np(a.dtype), kind="ExternalInput").ap())
    for i, shape in enumerate(_OUTS):
        args.append(nc.dram_tensor(f"out_{i}_dram", shape, F32, kind="ExternalOutput").ap())
    backbone_step(nc, *args)
    r = _run(nc, [arrays], core_ids=[0])
    return tuple(r.results[0][f"out_{i}_dram"] for i in range(len(_OUTS)))
```
